# Optimizing a Trainium2 kernel written in Bass

```python
import math
import jax, jax.numpy as jnp
from jax import lax
import numpy as np

D_MODEL = 1024
BATCH = 1
SEQ = 256
DEPTH = 2

BLOCK = 128
MLA_HEADS = 8
MLA_NOPE = 64
MLA_ROPE = 32
MLA_V = 64
MLA_Q_RANK = 256
MLA_KV_RANK = 128
ROPE_BASE = 10000.0
CONV_CH = 256
CONV_GROUPS = 4
CONV_WIDTH = 31
SWA_HEADS = 4
SWA_KV_HEADS = 2
SWA_HEAD_DIM = 64
WINDOW = 128
MLA_OUT = MLA_HEADS * MLA_V
SWA_OUT = SWA_HEADS * SWA_HEAD_DIM
D_MIX = MLA_OUT + CONV_CH + SWA_OUT
IN_SPLITS = (MLA_Q_RANK, MLA_KV_RANK, MLA_ROPE, 2 * CONV_CH,
             SWA_HEADS * SWA_HEAD_DIM, SWA_KV_HEADS * SWA_HEAD_DIM, SWA_KV_HEADS * SWA_HEAD_DIM)
D_IN = 256 + 128 + 32 + 512 + 256 + 128 + 128
N_SUBKEYS = 128
N_EXPERTS = N_SUBKEYS * N_SUBKEYS
PEER_HEADS = 8
PEER_QDIM = 256
PEER_TOPK = 16
DN_ALPHA = (2 * DEPTH) ** 0.25
DN_BETA = (8 * DEPTH) ** -0.25
EPS = 1e-6
ADA_SCALE = 0.1

kernel_name = "hybrid_mla_conformer_swa_peer_deepnorm"

def layer_norm(x, g, b):
    xf = x.astype(jnp.float32)
    mu = jnp.mean(xf, axis=-1, keepdims=True)
    var = jnp.mean(jnp.square(xf - mu), axis=-1, keepdims=True)
    return ((xf - mu) * lax.rsqrt(var + EPS)).astype(x.dtype) * g + b

def rms_norm(x, g):
    xf = x.astype(jnp.float32)
    return (xf * lax.rsqrt(jnp.mean(xf * xf, axis=-1, keepdims=True) + EPS)).astype(x.dtype) * g

def rope_tables(seq, dim, dtype):
    inv = 1.0 / (ROPE_BASE ** (jnp.arange(0, dim, 2, dtype=jnp.float32) / dim))
    ang = jnp.arange(seq, dtype=jnp.float32)[:, None] * inv[None, :]
    return jnp.cos(ang).astype(dtype), jnp.sin(ang).astype(dtype)

def apply_rope(t, cos, sin):
    half = t.shape[-1] // 2
    t1, t2 = t[..., :half], t[..., half:]
    return jnp.concatenate([t1 * cos - t2 * sin, t1 * sin + t2 * cos], axis=-1)

def mla_attention(c_q, c_kv, k_rope, g_q, w_uq, g_kv, w_ukv, cos, sin):
    B, S, _ = c_q.shape
    q = (rms_norm(c_q, g_q) @ w_uq).reshape(B, S, MLA_HEADS, MLA_NOPE + MLA_ROPE)
    q_nope = q[..., :MLA_NOPE]
    q_rope = apply_rope(q[..., MLA_NOPE:], cos[:, None, :], sin[:, None, :])
    k_rope = apply_rope(k_rope, cos, sin)
    kv = (rms_norm(c_kv, g_kv) @ w_ukv).reshape(B, S, MLA_HEADS, MLA_NOPE + MLA_V)
    k_nope, v = kv[..., :MLA_NOPE], kv[..., MLA_NOPE:]
    scale = (MLA_NOPE + MLA_ROPE) ** -0.5
    nb = S // BLOCK
    qn_b = q_nope.reshape(B, nb, BLOCK, MLA_HEADS, MLA_NOPE).transpose(1, 0, 2, 3, 4)
    qr_b = q_rope.reshape(B, nb, BLOCK, MLA_HEADS, MLA_ROPE).transpose(1, 0, 2, 3, 4)
    kpos = jnp.arange(S)

    def one_block(args):
        qn, qr, n = args
        s = (jnp.einsum('bqhd,bkhd->bhqk', qn, k_nope)
             + jnp.einsum('bqhr,bkr->bhqk', qr, k_rope)).astype(jnp.float32) * scale
        qpos = n * BLOCK + jnp.arange(BLOCK)
        s = jnp.where(kpos[None, :] <= qpos[:, None], s, -jnp.inf)
        p = jax.nn.softmax(s, axis=-1).astype(v.dtype)
        return jnp.einsum('bhqk,bkhd->bqhd', p, v)

    out = lax.map(one_block, (qn_b, qr_b, jnp.arange(nb)))
    return out.transpose(1, 0, 2, 3, 4).reshape(B, S, MLA_OUT)

def conformer_conv(u, w_dw, b_dw, g_ln, b_ln, w_pw, b_pw):
    a, gate = jnp.split(u, 2, axis=-1)
    h = a * jax.nn.sigmoid(gate)
    h = lax.conv_general_dilated(h, w_dw[:, None, :], window_strides=(1,),
                                 padding=[(CONV_WIDTH - 1, 0)],
                                 dimension_numbers=('NWC', 'WIO', 'NWC'),
                                 feature_group_count=CONV_CH) + b_dw
    h = jax.nn.silu(layer_norm(h, g_ln, b_ln))
    return h @ w_pw + b_pw

def swa_attention(q, k, v, sinks):
    B, S, _ = q.shape
    nb = S // BLOCK
    G = SWA_HEADS // SWA_KV_HEADS
    q = q.reshape(B, nb, BLOCK, SWA_KV_HEADS, G, SWA_HEAD_DIM)
    k = k.reshape(B, nb, BLOCK, SWA_KV_HEADS, SWA_HEAD_DIM)
    v = v.reshape(B, nb, BLOCK, SWA_KV_HEADS, SWA_HEAD_DIM)

    def with_prev(t):
        prev = jnp.pad(t, ((0, 0), (1, 0), (0, 0), (0, 0), (0, 0)))[:, :-1]
        return jnp.concatenate([prev, t], axis=2)

    kb, vb = with_prev(k), with_prev(v)
    s = jnp.einsum('bnqhgd,bnkhd->bnhgqk', q, kb).astype(jnp.float32) * (SWA_HEAD_DIM ** -0.5)
    i = jnp.arange(BLOCK)[:, None]
    j = jnp.arange(2 * BLOCK)[None, :]
    rel = i + BLOCK - j
    band = (rel >= 0) & (rel < WINDOW)
    valid = (jnp.arange(nb)[:, None, None] > 0) | (j >= BLOCK)[None]
    mask = band[None] & valid
    s = jnp.where(mask[None, :, None, None], s, -jnp.inf)
    sink = sinks.astype(jnp.float32).reshape(SWA_KV_HEADS, G)[None, None, :, :, None, None]
    m = jnp.maximum(jnp.max(s, axis=-1, keepdims=True), sink)
    p = jnp.exp(s - m)
    p = (p / (jnp.sum(p, axis=-1, keepdims=True) + jnp.exp(sink - m))).astype(vb.dtype)
    o = jnp.einsum('bnhgqk,bnkhd->bnqhgd', p, vb)
    return o.reshape(B, S, SWA_OUT)

def peer(h, w_pq, sub_keys, u_tab, v_tab):
    B, S, D = h.shape
    q = (h @ w_pq).reshape(B, S, PEER_HEADS, 2, PEER_QDIM // 2)
    sc = jnp.einsum('bshpd,hpnd->bshpn', q, sub_keys).astype(jnp.float32)
    s1, i1 = lax.top_k(sc[..., 0, :], PEER_TOPK)
    s2, i2 = lax.top_k(sc[..., 1, :], PEER_TOPK)
    cand = (s1[..., :, None] + s2[..., None, :]).reshape(B, S, PEER_HEADS, PEER_TOPK * PEER_TOPK)
    cidx = (i1[..., :, None] * N_SUBKEYS + i2[..., None, :]).reshape(B, S, PEER_HEADS, PEER_TOPK * PEER_TOPK)
    top_s, pos = lax.top_k(cand, PEER_TOPK)
    eidx = jnp.take_along_axis(cidx, pos, axis=-1)
    gate = jax.nn.softmax(top_s, axis=-1).astype(h.dtype)
    nb = S // BLOCK
    HK = PEER_HEADS * PEER_TOPK
    hb = h.reshape(B, nb, BLOCK, D).transpose(1, 0, 2, 3)
    eb = eidx.reshape(B, nb, BLOCK, HK).transpose(1, 0, 2, 3)
    gb = gate.reshape(B, nb, BLOCK, HK).transpose(1, 0, 2, 3)

    def one_block(args):
        xb, e, g = args
        a = jax.nn.gelu(jnp.einsum('bqd,bqkd->bqk', xb, u_tab[e]), approximate=False)
        return jnp.einsum('bqk,bqkd->bqd', g * a, v_tab[e])

    out = lax.map(one_block, (hb, eb, gb))
    return out.transpose(1, 0, 2, 3).reshape(B, S, D)

def setup_inputs(seed: int = 0) -> dict:
    key = jax.random.key(seed)
    ks = jax.random.split(key, 32)
    f32 = jnp.float32
    L, D = DEPTH, D_MODEL

    def nrm(k, shape, scale):
        return jax.random.normal(k, shape, f32) * scale

    def gain(k, shape):
        return 1.0 + 0.02 * jax.random.normal(k, shape, f32)

    return {
        "x": nrm(ks[0], (BATCH, SEQ, D), 1.0),
        "c": nrm(ks[1], (BATCH, D), 1.0),
        "w_ada": nrm(ks[2], (L, D, 6 * D), ADA_SCALE * D ** -0.5),
        "b_ada": nrm(ks[3], (L, 6 * D), 0.02),
        "w_in": nrm(ks[4], (L, D, D_IN), D ** -0.5),
        "g_q": gain(ks[5], (L, MLA_Q_RANK)),
        "w_uq": nrm(ks[6], (L, MLA_Q_RANK, MLA_HEADS * (MLA_NOPE + MLA_ROPE)), MLA_Q_RANK ** -0.5),
        "g_kv": gain(ks[7], (L, MLA_KV_RANK)),
        "w_ukv": nrm(ks[8], (L, MLA_KV_RANK, MLA_HEADS * (MLA_NOPE + MLA_V)), MLA_KV_RANK ** -0.5),
        "w_dw": nrm(ks[9], (L, CONV_WIDTH, CONV_CH), CONV_WIDTH ** -0.5),
        "b_dw": nrm(ks[10], (L, CONV_CH), 0.02),
        "g_conv": gain(ks[11], (L, CONV_CH)),
        "b_conv": nrm(ks[12], (L, CONV_CH), 0.02),
        "w_pw": nrm(ks[13], (L, CONV_CH, CONV_CH), CONV_CH ** -0.5),
        "b_pw": nrm(ks[14], (L, CONV_CH), 0.02),
        "sinks": nrm(ks[15], (L, SWA_HEADS), 1.0),
        "w_o": nrm(ks[16], (L, D_MIX, D), DN_BETA * D_MIX ** -0.5),
        "g_ln1": gain(ks[17], (L, D)),
        "b_ln1": nrm(ks[18], (L, D), 0.02),
        "w_pq": nrm(ks[19], (L, D, PEER_HEADS * PEER_QDIM), D ** -0.5),
        "sub_keys": nrm(ks[20], (L, PEER_HEADS, 2, N_SUBKEYS, PEER_QDIM // 2), (PEER_QDIM // 2) ** -0.5),
        "u_tab": nrm(ks[21], (L, N_EXPERTS, D), D ** -0.5),
        "v_tab": nrm(ks[22], (L, N_EXPERTS, D), DN_BETA),
        "g_ln2": gain(ks[23], (L, D)),
        "b_ln2": nrm(ks[24], (L, D), 0.02),
    }

def reference(x, c, w_ada, b_ada, w_in, g_q, w_uq, g_kv, w_ukv, w_dw, b_dw, g_conv, b_conv,
              w_pw, b_pw, sinks, w_o, g_ln1, b_ln1, w_pq, sub_keys, u_tab, v_tab, g_ln2, b_ln2):
    B, S, _ = x.shape
    cos, sin = rope_tables(S, MLA_ROPE, x.dtype)
    cs = jax.nn.silu(c)
    offsets = [int(o) for o in np.cumsum(IN_SPLITS)[:-1]]
    for l in range(DEPTH):
        mod = cs @ w_ada[l] + b_ada[l]
        sh1, sc1, gt1, sh2, sc2, gt2 = [m[:, None, :] for m in jnp.split(mod, 6, axis=-1)]

        h = x * (1.0 + sc1) + sh1
        proj = h @ w_in[l]
        c_q, c_kv, k_r, conv_u, q_s, k_s, v_s = jnp.split(proj, offsets, axis=-1)
        o_mla = mla_attention(c_q, c_kv, k_r, g_q[l], w_uq[l], g_kv[l], w_ukv[l], cos, sin)
        o_conv = conformer_conv(conv_u, w_dw[l], b_dw[l], g_conv[l], b_conv[l], w_pw[l], b_pw[l])
        o_swa = swa_attention(q_s, k_s, v_s, sinks[l])
        mix = jnp.concatenate([o_mla, o_conv, o_swa], axis=-1) @ w_o[l]
        x = layer_norm(DN_ALPHA * x + (1.0 + gt1) * mix, g_ln1[l], b_ln1[l])

        h = x * (1.0 + sc2) + sh2
        y = peer(h, w_pq[l], sub_keys[l], u_tab[l], v_tab[l])
        x = layer_norm(DN_ALPHA * x + (1.0 + gt2) * y, g_ln2[l], b_ln2[l])
    return x


_drawn_inputs = setup_inputs


def setup_inputs(seed=0):
    import zlib

    import numpy as np

    out = dict(_drawn_inputs(seed))
    spreads = {}
    factors = {'g_q': 4.278, 'g_kv': 3.329, 'g_conv': 2.699, 'b_conv': 3.123, 'sinks': 5.752}
    for name, (base, spread) in spreads.items():
        noise = np.random.default_rng([zlib.crc32(name.encode()), seed]).standard_normal(out[name].shape)
        drawn = base * np.exp(spread * noise) if base else spread * noise
        out[name] = __import__('jax').numpy.asarray(drawn.astype(out[name].dtype))
    for name, factor in factors.items():
        out[name] = (out[name] * factor).astype(out[name].dtype)
    return out
```

```python
import concourse.bass as bass
from concourse import mybir
from concourse.alu_op_type import AluOpType as ALU
from contextlib import ExitStack

F32 = mybir.dt.float32
U32 = mybir.dt.uint32
ACT = mybir.ActivationFunctionType
AX = mybir.AxisListType

P = 128
LAYERS = 2
D = 1024
SEQ = 256
TB = SEQ // P
KC = D // P
Q_RANK, KV_RANK, ROPE, CONV, TAPS = 256, 128, 32, 256, 31
MH, NOPE, MV = 8, 64, 64
QK = NOPE + ROPE
SH, SKV, SD = 4, 2, 64
AH = MH + SH
O_CQ, O_CKV, O_KR, O_CONV = 0, 256, 384, 416
O_QS, O_KS, O_VS = 928, 1184, 1312
D_IN = 1440
PROJ_N = D_IN // 3
CC = CONV // P
PAD = TAPS - 1
PH, PK, TOPK, NSUB = 8, 128, 16, 128
NEXP = NSUB * NSUB
GROUPS = PH * TB
ADA_N = 6 * D // GROUPS
ALPHA = float((2 * LAYERS) ** 0.25)
EPS = 1e-6
MLA_SCALE = float(QK) ** -0.5
SWA_SCALE = float(SD) ** -0.5
LOWEST = -3.0e38
MASKED = -1.0e30
SH1, SC1, GT1, SH2, SC2, GT2 = range(6)

RECTS = [(0, 1, 16), (1, 1, 8), (2, 2, 5), (4, 4, 3), (8, 8, 1)]
NCAND = sum(na * nb for _, na, nb in RECTS)

C_ID = 0
C_FULL = C_ID + P
C_BAND = C_FULL + 2 * P
C_COS = C_BAND + 2 * P
C_SIN = C_COS + TB * ROPE // 2
C_IOTA = C_SIN + TB * ROPE // 2
C_ONES = C_IOTA + NCAND
C_HALF = C_ONES + P
C_END = C_HALF + 2

UR = 4
VR = 4
SPAN = 4
PICKS = GROUPS * TOPK
U_TURN = PICKS + UR
V_TURN = PICKS + VR
DVE_STEPS = 35
PICK_PARTS = 8
SMALL_LOADS = 10
ADA_PE = 4
TICK = [None]


def hold(eng, sem, value):
    eng.wait_ge(sem, value)
    if not isinstance(value, int):
        eng.sem_inc(TICK[0], 1)


class Chain:

    def __init__(self, eng, sem):
        self.eng, self.sem, self.base, self.n = eng, sem, 0, 0

    def __call__(self, ins):
        ins.then_inc(self.sem, 1)
        self.n += 1

    def sync(self):
        hold(self.eng, self.sem, self.base + self.n)


def retrieval_loop(eng, body, chain=None, steps=0):
    spans = GROUPS // SPAN
    start = chain.base + chain.n if chain else 0
    with eng.Fori(0, spans - 1) as it:
        for j in range(SPAN):
            if chain:
                chain.base, chain.n = it * (SPAN * steps) + (start + j * steps), 0
            body(it, it * SPAN + j, j, False)
            if chain:
                assert chain.n == steps, chain.n
    if chain:
        chain.base, chain.n = start + (spans - 1) * SPAN * steps, 0
    for j in range(SPAN):
        body(spans - 1, (spans - 1) * SPAN + j, j, True)


def build(nc, x, c, w_ada, b_ada, w_in, g_q, w_uq, g_kv, w_ukv, w_dw, b_dw, g_conv, b_conv, w_pw,
          b_pw, sinks, w_o, g_ln1, b_ln1, w_pq, sub_keys, u_tab, v_tab, g_ln2, b_ln2, consts, out):
    ctx = ExitStack()
    with ctx:
        def sb(name, shape, dt=F32):
            return ctx.enter_context(nc.sbuf_tensor(name, shape, dt))

        cst = sb("cst", [P, C_END])
        win = sb("win", [P, KC * D_IN])
        ring = sb("ring", [P, UR + VR, D])
        wo = sb("wo", [P, KC * D])
        wpq = sb("wpq", [P, 2, KC * 2 * PK])
        mods = sb("mods", [P, 6, D])
        gt2 = sb("gt2", [P, D])
        xs = sb("xs", [P, TB, D])
        h = sb("h", [P, TB, D])
        hT = sb("hT", [P, KC, SEQ])
        skT = sb("skT", [P, 2 * PH, NSUB])
        ccol = sb("ccol", [P, KC])
        csb = sb("csb", [P, KC, P])
        brow = sb("brow", [1, 2, ADA_N])
        cols = sb("cols", [P, 12])
        sinkb = sb("sinkb", [P, SH])
        sinkd = sb("sinkd", [P, SH])
        wdT = sb("wdT", [P, CC, TAPS])
        stat = sb("stat", [P, 16])
        krot = sb("krot", [P, 4, ROPE // 2])
        rowmax = sb("rowmax", [P, AH])
        nmax = sb("nmax", [P, AH])
        rsum = sb("rsum", [P, AH])
        rinv = sb("rinv", [P, TB, AH])
        qrow = sb("qrow", [P, 2 * PK])
        qT2 = sb("qT2", [P, 2, P])
        sc = sb("sc", [P, TB, 2, NSUB])
        top = sb("top", [P, 2, TOPK])
        topi = sb("topi", [P, 2, TOPK], U32)
        topf = sb("topf", [P, 2, TOPK])
        cand = sb("cand", [P, NCAND])
        cide = sb("cide", [P, NCAND])
        pos = sb("pos", [P, TOPK], U32)
        posf = sb("posf", [P, TOPK])
        junk = sb("junk", [P, 512])
        eidf = sb("eidf", [P, TOPK])
        best = sb("best", [P, TB, TOPK])
        nbest = sb("nbest", [P, TB])
        warm = sb("warm", [P, TB])
        uidx = sb("uidx", [P, TB, TOPK], U32)
        vidx = sb("vidx", [P, TB, TOPK], U32)
        gexp = sb("gexp", [P, TB, TOPK])
        gsum = sb("gsum", [P, TB])
        ginv = sb("ginv", [P, TB])
        dots = sb("dots", [P, TB, TOPK])
        gel = sb("gel", [P, TB, TOPK])
        coef = sb("coef", [P, TB, TOPK])
        diag = sb("diag", [P, VR, P])

        ident = cst[:, C_ID:C_ID + P]
        full_mask = cst[:, C_FULL:C_FULL + 2 * P]
        band_mask = cst[:, C_BAND:C_BAND + 2 * P]
        own_mask = cst[:, C_FULL + P:C_FULL + 2 * P]
        ones_row = cst[0:1, C_ONES:C_ONES + P]
        ones_block = cst[:, C_ONES:C_ONES + P]
        zero_row = cst[0:1, C_FULL:C_FULL + P]
        any_row = cst[0:1, 0:512]
        iota_row = cst[:, C_IOTA:C_IOTA + NCAND]

        def view(t, lo, *shape):
            n = 1
            for d in shape:
                n *= d
            ap = t[:, lo:lo + n]
            if len(shape) == 2:
                return ap.rearrange("p (a b) -> p a b", a=shape[0])
            if len(shape) == 3:
                return ap.rearrange("p (a b c) -> p a b c", a=shape[0], b=shape[1])
            return ap

        def rows(ap, parts, shape):
            return ap[0:parts].rearrange("p (a b) -> p a b", a=shape)

        def over(ap, n):
            return ap.unsqueeze(1).to_broadcast([P, n, ap.shape[1]])

        def each(ap, n):
            return ap.unsqueeze(2).to_broadcast([P, ap.shape[1], n])

        win_w = view(win, 0, KC, D_IN)
        wo_w = view(wo, 0, KC, D)
        ada_w = [view(wo, t * KC * ADA_N, KC, ADA_N) for t in range(2)]
        ln2 = view(wo, 2 * KC * ADA_N, 2, D)
        ln1g, ln1b = mods[:, SC1, :], mods[:, SH1, :]
        wpq_w = [wpq[:, t, :].rearrange("p (k n) -> p k n", k=KC) for t in range(2)]
        small = wpq[:, :, :].rearrange("p s n -> p (s n)")
        wuq = view(small, 0, 2, MH * QK)
        wukv = view(small, 1536, MH * (NOPE + MV))
        wpw = view(small, 2560, CC, CONV)
        rr = ring[:, :, :].rearrange("p s n -> p (s n)")
        proj = view(rr, 0, TB, D_IN)
        qrows = [view(rr, 2880 + t * MH * QK, MH, QK) for t in range(TB)]
        krows = [view(rr, 4416 + t * MH * QK, MH, QK) for t in range(TB)]
        vrows = [view(rr, 5952 + t * MH * MV, MH, MV) for t in range(TB)]
        pT = view(rr, 2880, AH, 2, P)
        lift = view(rr, 7168, D)
        qTh = view(win, 0, MH, SEQ)
        kTh = view(win, 2048, MH, SEQ)
        qsT = view(win, 4096, SH, SEQ)
        ksT = view(win, 5120, SKV, SEQ)
        S = view(win, 5632, AH, 2 * P)
        hc = view(win, 8704, CC, PAD + SEQ)
        cacc = view(win, 9276, CC, SEQ)
        crow = view(win, 9788, TB, CONV)
        cqT = view(win, 10300, 2, SEQ)
        ckvT = view(win, 10812, SEQ)
        wdraw = view(win, 11068, CONV)
        orow, oT = h, hT
        hnT = cacc
        sk_raw = view(win, 0, 2 * PH, PK)
        eq = view(junk, 0, TOPK // 2, NCAND)

        pb = [ctx.enter_context(nc.psum_tensor(f"pb{i}", [P, 512], F32)) for i in range(8)]
        Y = [(pb[0], pb[1]), (pb[2], pb[3])]
        Q_BANK, QS_BANK, ADA_BANK = pb[4], pb[5], (pb[6], pb[7])

        names = """tick dve_chain consts_in c_in x_in cs_ready csb_ready ada_in0 ada_in1 ada_made terms_ready
        ada_out win_in small_in wo_in ln1_in ln2_in skr_in wdr_in h_ready hT_made hT_out proj_made
        proj_out sw_made sw_out rms_ready glu_sig glu_ready cn_made cn_out qkv_made qkv_out rope_ready
        hq_made hq_out conv_in_made conv_in_out wd_made wd_out conv_ready conv_row_made conv_norm
        conv_col_made conv_act conv_pw_made conv_pw_out sc_made mask_out max_ready exp_out pT_made
        pT_out o_made o_out oT_made oT_out mix_made ln1_done h2_ready h2T_made h2T_out sk_made sk_out
        gt2_kept gained var_ready root_out q_made q_out qT_made qT_out s_made s_out wpq_in0 wpq_in1 idx_ready picks_ready
        gate_out u_used gelu_out coef_ready vidx_ready diag_ready v_used y_made ln2_done
        out_stored""".split()
        s = {n: ctx.enter_context(nc.semaphore(n)) for n in names}
        TICK[0] = s["tick"]
        u_in = [ctx.enter_context(nc.semaphore(f"u_in{i}")) for i in range(UR)]
        v_in = [ctx.enter_context(nc.semaphore(f"v_in{i}")) for i in range(VR)]

        block = ctx.enter_context(nc.Block())
        u_flat = u_tab.rearrange("l e d -> (l e) d")
        v_flat = v_tab.rearrange("l e d -> (l e) d")

        @block.sync
        def _(sp):
            sp.dma_start(cst[:, :], consts).then_inc(s["consts_in"], 16)
            sp.dma_start(ccol[:, :], c.rearrange("b (k p) -> p (b k)", p=P), allow_slow_non_contiguous=True).then_inc(s["c_in"], 16)

            def ada_load(l, i, slot):
                cut = bass.ds(i * ADA_N, ADA_N)
                sp.dma_start(ada_w[slot], w_ada[l].rearrange("(k p) n -> p k n", p=P)[:, :, cut]
                             ).then_inc(s[f"ada_in{slot}"], 16)
                sp.dma_start(brow[0:1, slot, :], b_ada[l:l + 1, cut]).then_inc(s[f"ada_in{slot}"], 16)

            def load_small(l):
                got = s["small_in"]
                sp.dma_start(wuq, w_uq[l].rearrange("(k p) n -> p k n", p=P)).then_inc(got, 16)
                sp.dma_start(wukv, w_ukv[l]).then_inc(got, 16)
                sp.dma_start(wpw, w_pw[l].rearrange("(k p) n -> p k n", p=P)).then_inc(got, 16)
                sp.dma_start(cols[:, 0:2], g_q[l].rearrange("(k p) -> p k", p=P), allow_slow_non_contiguous=True).then_inc(got, 16)
                sp.dma_start(cols[:, 2:3], g_kv[l].rearrange("(k p) -> p k", p=P), allow_slow_non_contiguous=True).then_inc(got, 16)
                for j, w in enumerate((b_dw, g_conv, b_conv, b_pw)):
                    sp.dma_start(cols[:, 3 + 2 * j:5 + 2 * j], w[l].rearrange("(k p) -> p k", p=P),
                                 allow_slow_non_contiguous=True).then_inc(got, 16)
                sp.dma_start(sinkb[:, :], sinks[l:l + 1, :].to_broadcast([P, SH])).then_inc(got, 16)

            def wpq_load(l, hd):
                src = w_pq[l].rearrange("(k p) n -> p k n", p=P)[:, :, hd * 2 * PK:(hd + 1) * 2 * PK]
                sp.dma_start(wpq_w[hd % 2], src).then_inc(s[f"wpq_in{hd % 2}"], 16)

            for j in range(2):
                ada_load(0, j, j)
            with sp.Fori(0, GROUPS // 2 - 1) as it:
                for j in range(2):
                    hold(sp, s["ada_made"], it * 2 + (j + 1))
                    ada_load(0, it * 2 + (2 + j), j)
            sp.dma_start(xs[:, :, :], x[0].rearrange("(t p) d -> p t d", p=P)).then_inc(s["x_in"], 16)
            sp.dma_start(win_w, w_in[0].rearrange("(k p) n -> p k n", p=P)).then_inc(s["win_in"], 16)
            for l in range(LAYERS):
                if l:
                    sp.wait_ge(s["s_made"], GROUPS * l)
                load_small(l)
                sp.wait_ge(s["ada_made"], GROUPS * (l + 1))
                if l:
                    sp.wait_ge(s["ln2_done"], TB * l)
                sp.dma_start(wo_w, w_o[l].rearrange("(k p) n -> p k n", p=P)).then_inc(s["wo_in"], 16)
                sp.wait_ge(s["h_ready"], TB * (l + 1))
                sp.dma_start(ln1g, g_ln1[l:l + 1, :].to_broadcast([P, D])).then_inc(s["ln1_in"], 16)
                sp.dma_start(ln1b, b_ln1[l:l + 1, :].to_broadcast([P, D])).then_inc(s["ln1_in"], 16)
                sp.wait_ge(s["proj_made"], 3 * TB * (l + 1))
                sp.dma_start(wdraw[0:TAPS, :], w_dw[l]).then_inc(s["wdr_in"], 16)
                sp.wait_ge(s["sc_made"], 9 * (l + 1))
                sp.dma_start(sk_raw, sub_keys[l].rearrange("h q n d -> n (h q) d")).then_inc(s["skr_in"], 16)
                sp.wait_ge(s["mix_made"], TB * (l + 1))
                for hd in range(2):
                    wpq_load(l, hd)
                for j, w in enumerate((g_ln2, b_ln2)):
                    sp.dma_start(ln2[:, j, :], w[l:l + 1, :].to_broadcast([P, D])).then_inc(s["ln2_in"], 16)
                ahead = l + 1 < LAYERS
                if ahead:
                    for j in range(2):
                        ada_load(l + 1, j, j)
                for hd in range(2, PH):
                    sp.wait_ge(s["q_made"], GROUPS * l + TB * (hd - 1))
                    wpq_load(l, hd)
                    if ahead:
                        for i in (2 * hd - 2, 2 * hd - 1):
                            sp.wait_ge(s["ada_made"], GROUPS * (l + 1) + i - 1)
                            ada_load(l + 1, i, i % 2)
                if ahead:
                    for i in (GROUPS - 2, GROUPS - 1):
                        sp.wait_ge(s["ada_made"], GROUPS * (l + 1) + i - 1)
                        ada_load(l + 1, i, i % 2)
                    sp.wait_ge(s["sk_made"], 4 * (l + 1))
                    sp.dma_start(win_w, w_in[l + 1].rearrange("(k p) n -> p k n", p=P)).then_inc(s["win_in"], 16)
            for t in range(TB):
                sp.wait_ge(s["ln2_done"], TB * (LAYERS - 1) + t + 1)
                sp.dma_start(out[0, t * P:(t + 1) * P, :], xs[:, t, :]).then_inc(s["out_stored"], 16)
            sp.wait_ge(s["out_stored"], 16 * TB)

        @block.gpsimd
        def _(pool):
            asked = gained = 0

            def reciprocal_roots(lo, n, times):
                nonlocal asked
                for _ in range(times):
                    asked += 1
                    pool.wait_ge(s["var_ready"], asked)
                    nc.gpsimd.tensor_tensor(stat[:, lo:lo + n], stat[:, lo:lo + n],
                                            cst[:, C_HALF:C_HALF + n], ALU.pow).then_inc(s["root_out"], 1)

            def gain_and_offset(t, gain, offset, done):
                nonlocal gained
                nc.gpsimd.tensor_tensor(xs[:, t, :], xs[:, t, :], gain, ALU.mult).then_inc(s["gained"], 1)
                gained += 1
                pool.wait_ge(s["gained"], gained)
                nc.gpsimd.tensor_tensor(xs[:, t, :], xs[:, t, :], offset, ALU.add).then_inc(done, 1)

            for l in range(LAYERS):
                reciprocal_roots(0, 2, TB)
                reciprocal_roots(13, 1, TB)
                reciprocal_roots(13, 1, TB)
                for t in range(TB):
                    pool.wait_ge(s["h2_ready"], TB * l + t + 1)
                    gain_and_offset(t, ln1g, ln1b, s["ln1_done"])

                def gather_u(i, t, k):
                    hold(pool, s["u_used"], i * TOPK + (U_TURN * l + k + 1))
                    nc.gpsimd.indirect_dma_start(
                        out=ring[:, k % UR, :], out_offset=None, in_=u_flat,
                        in_offset=bass.IndirectOffsetOnAxis(ap=uidx[:, t, k:k + 1], axis=0)
                    ).then_inc(u_in[k % UR], 16)

                def gather_v(i, t, k):
                    hold(pool, s["v_used"], i * TOPK + (V_TURN * l + k + 1))
                    nc.gpsimd.indirect_dma_start(
                        out=ring[:, UR + k % VR, :], out_offset=None, in_=v_flat,
                        in_offset=bass.IndirectOffsetOnAxis(ap=vidx[:, t, k:k + 1], axis=0)
                    ).then_inc(v_in[k % VR], 16)

                def body(it, i, j, last):
                    more = not (last and j == SPAN - 1)
                    if more:
                        hold(pool, s["idx_ready"], i + (GROUPS * l + 2))
                    hold(pool, s["vidx_ready"], i + (GROUPS * l + 1))
                    for k in range(TOPK):
                        if more:
                            gather_u(i + 1, (j + 1) % TB, k)
                        gather_v(i, j % TB, k)

                pool.wait_ge(s["idx_ready"], GROUPS * l + 1)
                for k in range(TOPK):
                    gather_u(0, 0, k)
                retrieval_loop(pool, body)
                reciprocal_roots(13, 1, TB)
                if l + 1 < LAYERS:
                    for t in range(TB):
                        pool.wait_ge(s["h_ready"], TB * (l + 1) + t + 1)
                        gain_and_offset(t, ln2[:, 0, :], ln2[:, 1, :], s["ln2_done"])

        @block.scalar
        def _(act):
            copy = nc.scalar.copy
            f = nc.scalar.activation

            def ada_out(l, i, j):
                hold(act, s["ada_made"], i + (GROUPS * l + 1))
                flat = mods[:, :, :].rearrange("p a n -> p (a n)")
                f(flat[:, bass.ds(i * ADA_N, ADA_N)], ADA_BANK[j % 2][:, 0:ADA_N], ACT.Copy
                  ).then_inc(s["ada_out"], 1)

            act.sem_inc(s["ada_out"], 2)
            act.wait_ge(s["c_in"], 16)
            f(ccol[:, :], ccol[:, :], ACT.Silu).then_inc(s["cs_ready"], 1)
            with act.Fori(0, GROUPS // 2) as it:
                for j in range(2):
                    ada_out(0, it * 2 + j, j)

            for l in range(LAYERS):
                for b in range(4):
                    act.wait_ge(s["hT_made"], 4 * l + b + 1)
                    t, half = b // 2, b % 2
                    copy(hT[:, 4 * half:4 * half + 4, t * P:(t + 1) * P], rows(pb[b], P, 4)
                         ).then_inc(s["hT_out"], 1)
                for b in range(6):
                    act.wait_ge(s["proj_made"], 6 * l + b + 1)
                    t, n = b // 3, b % 3
                    copy(proj[:, t, n * PROJ_N:(n + 1) * PROJ_N], pb[(4 + b) % 8 if b < 4 else b - 4][:, 0:PROJ_N]
                         ).then_inc(s["proj_out"], 1)
                act.wait_ge(s["proj_out"], 6 * (l + 1))
                gate = proj[:, :, O_CONV + CONV:O_CONV + 2 * CONV]
                f(gate, gate, ACT.Sigmoid).then_inc(s["glu_sig"], 1)
                act.wait_ge(s["small_in"], 16 * SMALL_LOADS * (l + 1))
                for t in range(TB):
                    cut = slice(t * P, (t + 1) * P)
                    act.wait_ge(s["sw_made"], 4 * l + 2 * t + 1)
                    copy(qsT[0:SD, :, cut], rows(pb[4 + 2 * t], SD, 4)).then_inc(s["sw_out"], 1)
                    act.wait_ge(s["sw_made"], 4 * l + 2 * t + 2)
                    copy(ksT[0:SD, :, cut], rows(pb[5 + 2 * t][:, 0:2 * P], SD, 2)).then_inc(s["sw_out"], 1)
                for t in range(TB):
                    cut = slice(t * P, (t + 1) * P)
                    act.wait_ge(s["cn_made"], TB * l + t + 1)
                    f(cqT[:, 0, cut], pb[2 + t][:, 0:P], ACT.Copy, scale=cols[:, 0:1])
                    f(cqT[:, 1, cut], pb[2 + t][:, P:2 * P], ACT.Copy, scale=cols[:, 1:2])
                    f(ckvT[:, cut], pb[2 + t][:, 2 * P:3 * P], ACT.Copy, scale=cols[:, 2:3]
                      ).then_inc(s["cn_out"], 1)
                act.wait_ge(s["conv_in_made"], l + 1)
                copy(hc[:, :, PAD:PAD + SEQ], rows(pb[0], P, 2)).then_inc(s["conv_in_out"], 1)
                act.wait_ge(s["wd_made"], l + 1)
                copy(wdT[:, :, :], rows(pb[1][:, 0:2 * P], P, 2)[:, :, 0:TAPS]).then_inc(s["wd_out"], 1)
                for t in range(TB):
                    bank = pb[4:8] if t == 0 else pb[0:4]
                    for n in range(2):
                        act.wait_ge(s["qkv_made"], 8 * l + 4 * t + n + 1)
                        copy(qrows[t][:, 4 * n:4 * n + 4, :], rows(bank[n][:, 0:4 * QK], P, 4)
                             ).then_inc(s["qkv_out"], 1)
                    for n in range(2):
                        act.wait_ge(s["qkv_made"], 8 * l + 4 * t + n + 3)
                        kv = rows(bank[2 + n], P, 4)
                        copy(krows[t][:, 4 * n:4 * n + 4, 0:NOPE], kv[:, :, 0:NOPE]).then_inc(s["qkv_out"], 1)
                        copy(vrows[t][:, 4 * n:4 * n + 4, :], kv[:, :, NOPE:NOPE + MV]).then_inc(s["qkv_out"], 1)
                for t in range(TB):
                    bank = pb[4:8] if t == 0 else pb[0:4]
                    for n in range(4):
                        act.wait_ge(s["hq_made"], 8 * l + 4 * t + n + 1)
                        to = (qTh, kTh)[n // 2]
                        copy(to[0:QK, 4 * (n % 2):4 * (n % 2) + 4, t * P:(t + 1) * P], rows(bank[n], QK, 4)
                             ).then_inc(s["hq_out"], 1)
                for t in range(TB):
                    lo = P if t == 0 else 0
                    act.wait_ge(s["max_ready"], TB * l + t + 1)
                    f(sinkd[:, :], sinkd[:, :], ACT.Exp)
                    for a in range(AH):
                        e = f(S[:, a, lo:2 * P], S[:, a, lo:2 * P], ACT.Exp, bias=nmax[:, a:a + 1],
                              scale=MLA_SCALE if a < MH else SWA_SCALE, accum_out=rsum[:, a:a + 1])
                    e.then_inc(s["exp_out"], 1)
                    for n in range(3 if t == 0 else 6):
                        act.wait_ge(s["pT_made"], 9 * l + 3 * t + n + 1)
                        if t == 0:
                            copy(pT[:, 4 * n:4 * n + 4, 1, :], rows(pb[n], P, 4)).then_inc(s["pT_out"], 1)
                        else:
                            src = pb[3 + n] if n < 5 else pb[2]
                            copy(pT[:, 2 * n:2 * n + 2, :, :].rearrange("p a b c -> p (a b c)"), src[:, :]
                                 ).then_inc(s["pT_out"], 1)
                act.wait_ge(s["conv_col_made"], l + 1)
                for n in range(CC):
                    e = f(hnT[:, n, :], pb[2][:, n * SEQ:(n + 1) * SEQ], ACT.Silu,
                          bias=cols[:, 7 + n:8 + n], scale=cols[:, 5 + n:6 + n])
                e.then_inc(s["conv_act"], 1)
                act.wait_ge(s["oT_made"], 4 * (l + 1))
                for b in range(4):
                    t, n = b // 2, b % 2
                    cut = slice(t * P, (t + 1) * P)
                    if n == 0:
                        e = copy(oT[:, 0:4, cut], rows(pb[3 + b], P, 4))
                    else:
                        e = copy(oT[:, 6:8, cut], rows(pb[3 + b][:, 0:2 * P], P, 2))
                    e.then_inc(s["oT_out"], 1)
                act.wait_ge(s["conv_pw_made"], l + 1)
                for n in range(CC):
                    e = f(oT[:, 4 + n, :], pb[7][:, n * SEQ:(n + 1) * SEQ], ACT.Identity, bias=cols[:, 9 + n:10 + n])
                e.then_inc(s["conv_pw_out"], 1)
                for b in range(4):
                    act.wait_ge(s["sk_made"], 4 * l + b + 1)
                    copy(skT[:, 4 * b:4 * b + 4, :], rows(pb[4 + b], P, 4)).then_inc(s["sk_out"], 1)

                def query_out(g):
                    hold(act, s["q_made"], g + (GROUPS * l + 1))
                    copy(qrow[:, :], Q_BANK[:, 0:2 * PK]).then_inc(s["q_out"], 1)
                    hold(act, s["qT_made"], g + (GROUPS * l + 1))
                    copy(qT2[:, :, :], rows(QS_BANK[:, 0:2 * P], P, 2)).then_inc(s["qT_out"], 1)

                def scores_out(g, t):
                    hold(act, s["s_made"], g + (GROUPS * l + 1))
                    copy(sc[:, t, :, :], rows(QS_BANK[:, 2 * P:4 * P], P, 2)).then_inc(s["s_out"], 1)

                def gate_exp(g, t):
                    hold(act, s["picks_ready"], g + (GROUPS * l + 1))
                    f(gexp[:, t, :], best[:, t, :], ACT.Exp, bias=nbest[:, t:t + 1],
                      accum_out=gsum[:, t:t + 1]).then_inc(s["gate_out"], 1)
                    f(warm[:, t:t + 1], cst[:, C_HALF:C_HALF + 1], ACT.Gelu)

                def gelu(g, t):
                    hold(act, s["u_used"], g * TOPK + (U_TURN * l + UR + TOPK))
                    f(gel[:, t, :], dots[:, t, :], ACT.Gelu).then_inc(s["gelu_out"], 1)

                def diagonals(i, t, ks):
                    for k in ks:
                        hold(act, s["v_used"], i * TOPK + (V_TURN * l + k + 1))
                        f(diag[:, k % VR, :], ident, ACT.Copy, scale=coef[:, t, k:k + 1]
                          ).then_inc(s["diag_ready"], 1)

                def body(it, i, j, last):
                    t = j % TB
                    hold(act, s["coef_ready"], i + (GROUPS * l + 1))
                    asks = not (last and j + 3 >= SPAN)
                    diagonals(i, t, range(12))
                    if asks:
                        query_out(i + 3)
                    diagonals(i, t, (12,))
                    if asks:
                        hold(act, s["idx_ready"], i + (GROUPS * l + 2))
                        scores_out(i + 3, (j + 3) % TB)
                    diagonals(i, t, (13,))
                    if not (last and j + 2 >= SPAN):
                        gate_exp(i + 2, t)
                    diagonals(i, t, (14, 15))
                    if l + 1 < LAYERS:
                        ada_out(l + 1, i, j)
                    if not (last and j + 1 >= SPAN):
                        gelu(i + 1, (j + 1) % TB)

                for g in range(3):
                    t = g % TB
                    if g < TB:
                        for half in range(2):
                            act.wait_ge(s["h2T_made"], 4 * l + 2 * t + half + 1)
                            copy(hT[:, 4 * half:4 * half + 4, t * P:(t + 1) * P], rows(pb[2 * t + half], P, 4)
                                 ).then_inc(s["h2T_out"], 1)
                    query_out(g)
                    if g == 2:
                        act.wait_ge(s["idx_ready"], GROUPS * l + 1)
                    scores_out(g, t)
                gate_exp(0, 0)
                gate_exp(1, 1)
                gelu(0, 0)
                if l + 1 < LAYERS:
                    act.wait_ge(s["gt2_kept"], l + 1)
                    act.wait_ge(s["ln1_done"], TB * (l + 1))
                retrieval_loop(act, body)

        @block.vector
        def _(dve):
            v = nc.vector
            chain = Chain(dve, s["dve_chain"])
            roots = [0]

            def layer_norm(t, src_bank, gate, to, gain, offset, done):
                xt, ht = xs[:, t, :], h[:, t, :]
                for n in range(2):
                    cut = slice(n * 512, (n + 1) * 512)
                    chain(v.scalar_tensor_tensor(ht[:, cut], gate[:, cut], 1.0, src_bank[n][:, :],
                                                 ALU.add, ALU.mult))
                chain.sync()
                chain(v.scalar_tensor_tensor(xt, xt, ALPHA, ht, ALU.mult, ALU.add))
                chain.sync()
                norm_stats(xt, D)
                chain(v.tensor_scalar(xt, xt, stat[:, 12:13], stat[:, 13:14], ALU.subtract, ALU.mult))
                chain.sync()
                chain(v.tensor_tensor(to[:, t, :], xt, gain, ALU.mult))
                chain.sync()
                v.tensor_tensor(to[:, t, :], to[:, t, :], offset, ALU.add).then_inc(done, 1)

            def fold(scale, shift, gain, offset, lift):
                scale, shift = mods[:, scale, :], mods[:, shift, :]
                chain(v.scalar_tensor_tensor(lift, scale, 1.0, offset, ALU.add, ALU.mult))
                chain.sync()
                chain(v.tensor_tensor(shift, shift, lift, ALU.add))
                chain(v.scalar_tensor_tensor(scale, scale, 1.0, gain, ALU.add, ALU.mult))
                chain.sync()

            def norm_stats(src, n):
                parts = max(1, n // 512)
                for q in range(parts):
                    chain(v.bn_stats(stat[:, 6 * q:6 * q + 6], src[:, q * (n // parts):(q + 1) * (n // parts)]))
                chain.sync()
                chain(v.bn_aggr(stat[:, 12:14], stat[:, 0:6 * parts]))
                chain.sync()
                v.tensor_scalar(stat[:, 13:14], stat[:, 13:14], EPS, None, ALU.add).then_inc(s["var_ready"], 1)
                roots[0] += 1
                dve.wait_ge(s["root_out"], roots[0])

            def modulate(t, scale, shift, ready):
                chain(v.scalar_tensor_tensor(h[:, t, :], mods[:, scale, :], 1.0, xs[:, t, :], ALU.add, ALU.mult))
                chain.sync()
                v.tensor_tensor(h[:, t, :], h[:, t, :], mods[:, shift, :], ALU.add).then_inc(ready, 1)

            dve.wait_ge(s["consts_in"], 16)
            dve.wait_ge(s["cs_ready"], 1)
            v.tensor_copy(csb[:, :, :], each(ccol[:, :], P)).then_inc(s["csb_ready"], 1)
            def terms(i, j, turn):
                hold(dve, s[f"ada_in{j % 2}"], turn)
                to = h[:, j % 2, 0:ADA_N]
                for k in range(ADA_PE, KC):
                    if k == ADA_PE:
                        e = v.tensor_scalar(to, ada_w[j % 2][:, k, :], ccol[:, k:k + 1], None, ALU.mult)
                    else:
                        chain.sync()
                        e = v.scalar_tensor_tensor(to, ada_w[j % 2][:, k, :], ccol[:, k:k + 1], to, ALU.mult, ALU.add)
                    if k < KC - 1:
                        chain(e)
                    else:
                        e.then_inc(s["terms_ready"], 1)

            with dve.Fori(0, GROUPS // 2) as it:
                for j in range(2):
                    chain.base, chain.n = (it * 2 + j) * (KC - ADA_PE - 1), 0
                    terms(it * 2 + j, j, it * 32 + 32)
            chain.base, chain.n = GROUPS * (KC - ADA_PE - 1), 0
            dve.wait_ge(s["x_in"], 16)

            for l in range(LAYERS):
                if l == 0:
                    dve.wait_ge(s["ada_out"], 2 + GROUPS)
                    for t in range(TB):
                        modulate(t, SC1, SH1, s["h_ready"])
                dve.wait_ge(s["ada_out"], 2 + GROUPS * (l + 1))
                dve.wait_ge(s["ln1_in"], 32 * (l + 1))
                fold(SC2, SH2, ln1g, ln1b, lift)
                v.tensor_copy(gt2[:, :], mods[:, GT2, :]).then_inc(s["gt2_kept"], 1)
                for t in range(TB):
                    dve.wait_ge(s["proj_out"], 6 * l + 3 * t + 1)
                    if t == 0:
                        chain.sync()
                    parts = ((O_CQ, Q_RANK, 0), (O_CKV, KV_RANK, 1))
                    for lo, n, q in parts:
                        p_ = proj[:, t, lo:lo + n]
                        chain(v.scalar_tensor_tensor(junk[:, lo:lo + n], p_, 1.0, p_, ALU.mult, ALU.mult,
                                                     accum_out=stat[:, q:q + 1]))
                    chain.sync()
                    for lo, n, q in parts:
                        e = v.tensor_scalar(stat[:, q:q + 1], stat[:, q:q + 1], 1.0 / n, EPS, ALU.mult, ALU.add)
                        if q == 0:
                            chain(e)
                        else:
                            e.then_inc(s["var_ready"], 1)
                    roots[0] += 1
                    dve.wait_ge(s["root_out"], roots[0])
                    for lo, n, q in parts:
                        p_ = proj[:, t, lo:lo + n]
                        e = v.tensor_scalar(p_, p_, stat[:, q:q + 1], None, ALU.mult)
                        if q == 0:
                            chain(e)
                        else:
                            e.then_inc(s["rms_ready"], 1)
                    dve.wait_ge(s["rms_ready"], TB * l + t + 1)
                dve.wait_ge(s["glu_sig"], l + 1)
                a_ = proj[:, :, O_CONV:O_CONV + CONV]
                v.tensor_tensor(a_, a_, proj[:, :, O_CONV + CONV:O_CONV + 2 * CONV], ALU.mult
                                ).then_inc(s["glu_ready"], 1)
                chain(v.memset(hc[:, :, 0:PAD], 0.0))
                half = ROPE // 2
                for t in range(TB):
                    cos = cst[:, C_COS + t * half:C_COS + (t + 1) * half]
                    sin = cst[:, C_SIN + t * half:C_SIN + (t + 1) * half]
                    k1 = proj[:, t, O_KR:O_KR + half]
                    k2 = proj[:, t, O_KR + half:O_KR + ROPE]
                    for q, (a_, b_) in enumerate(((k1, cos), (k2, sin), (k1, sin), (k2, cos))):
                        chain(v.tensor_tensor(krot[:, q, :], a_, b_, ALU.mult))
                    chain.sync()
                    chain(v.tensor_tensor(krot[:, 0, :], krot[:, 0, :], krot[:, 1, :], ALU.subtract))
                    chain(v.tensor_tensor(krot[:, 2, :], krot[:, 2, :], krot[:, 3, :], ALU.add))
                    chain.sync()
                    chain(v.tensor_copy(krows[t][:, :, NOPE:NOPE + half], over(krot[:, 0, :], MH)))
                    chain(v.tensor_copy(krows[t][:, :, NOPE + half:QK], over(krot[:, 2, :], MH)))
                    chain.sync()
                    dve.wait_ge(s["qkv_out"], 12 * l + 6 * t + 2)
                    q1 = qrows[t][:, :, NOPE:NOPE + half]
                    q2 = qrows[t][:, :, NOPE + half:QK]
                    tmp = [rows(junk[:, q * MH * half:(q + 1) * MH * half], P, MH) for q in range(4)]
                    for q, (a_, b_) in enumerate(((q1, cos), (q2, sin), (q1, sin), (q2, cos))):
                        chain(v.tensor_tensor(tmp[q], a_, over(b_, MH), ALU.mult))
                    chain.sync()
                    chain(v.tensor_tensor(q1, tmp[0], tmp[1], ALU.subtract))
                    v.tensor_tensor(q2, tmp[2], tmp[3], ALU.add).then_inc(s["rope_ready"], 1)
                    dve.wait_ge(s["rope_ready"], TB * l + t + 1)

                def taps(k0, k1):
                    for k in range(k0, k1):
                        for n in range(CC):
                            src = hc[:, n, k:k + SEQ]
                            if k == 0:
                                chain(v.tensor_scalar(cacc[:, n, :], src, wdT[:, n, 0:1], cols[:, 3 + n:4 + n],
                                                      ALU.mult, ALU.add))
                            else:
                                chain(v.scalar_tensor_tensor(cacc[:, n, :], src, wdT[:, n, k:k + 1],
                                                             cacc[:, n, :], ALU.mult, ALU.add))
                        chain.sync()

                dve.wait_ge(s["conv_in_out"], l + 1)
                dve.wait_ge(s["wd_out"], l + 1)
                dve.wait_ge(s["small_in"], 16 * SMALL_LOADS * (l + 1))
                taps(0, 16)

                for t in range(TB):
                    if t:
                        dve.wait_ge(s["pT_made"], 9 * l + 3)
                    for n in range(3 if t == 0 else 6):
                        dve.wait_ge(s["sc_made"], 9 * l + 3 * t + n + 1)
                        if t == 0:
                            e = v.tensor_tensor(S[:, 4 * n:4 * n + 4, P:2 * P], rows(pb[n], P, 4),
                                                over(own_mask, 4), ALU.add)
                        else:
                            src = pb[3 + n] if n < 5 else pb[2]
                            e = v.tensor_tensor(S[:, 2 * n:2 * n + 2, :], rows(src, P, 2),
                                                over(full_mask if n < 4 else band_mask, 2), ALU.add)
                        e.then_inc(s["mask_out"], 1)
                    dve.wait_ge(s["mask_out"], 9 * l + (3 if t == 0 else 9))
                    chain(v.tensor_reduce(rowmax[:, :], S[:, :, P if t == 0 else 0:2 * P], AX.X, ALU.max))
                    chain.sync()
                    chain(v.tensor_scalar(nmax[:, 0:MH], rowmax[:, 0:MH], -MLA_SCALE, None, ALU.mult))
                    chain(v.scalar_tensor_tensor(rowmax[:, MH:AH], rowmax[:, MH:AH], SWA_SCALE, sinkb[:, :],
                                                 ALU.mult, ALU.max))
                    chain.sync()
                    chain(v.tensor_scalar(nmax[:, MH:AH], rowmax[:, MH:AH], -1.0, None, ALU.mult))
                    v.tensor_tensor(sinkd[:, :], sinkb[:, :], rowmax[:, MH:AH], ALU.subtract
                                    ).then_inc(s["max_ready"], 1)
                    taps(16 if t == 0 else 24, 24 if t == 0 else TAPS)
                    dve.wait_ge(s["exp_out"], TB * l + t + 1)
                    chain(v.tensor_tensor(rsum[:, MH:AH], rsum[:, MH:AH], sinkd[:, :], ALU.add))
                    chain.sync()
                    chain(v.reciprocal(rinv[:, t, :], rsum[:, :]))
                    chain.sync()
                    dve.wait_ge(s["o_made"], TB * l + t + 1)
                    chain(v.tensor_tensor(rows(orow[:, t, 0:512], P, MH), rows(pb[0], P, MH),
                                          each(rinv[:, t, 0:MH], MV), ALU.mult))
                    v.tensor_tensor(rows(orow[:, t, 512:768], P, SH), rows(pb[1][:, 0:256], P, SH),
                                    each(rinv[:, t, MH:AH], SD), ALU.mult).then_inc(s["o_out"], 1)
                chain.sync()
                dve.wait_ge(s["conv_row_made"], l + 1)
                for t in range(TB):
                    norm_stats(pb[7][:, t * CONV:(t + 1) * CONV], CONV)
                    chain(v.tensor_scalar(crow[:, t, :], pb[7][:, t * CONV:(t + 1) * CONV], stat[:, 12:13],
                                          stat[:, 13:14], ALU.subtract, ALU.mult))
                    chain.sync()
                dve.sem_inc(s["conv_norm"], 1)
                dve.wait_ge(s["oT_made"], 4 * (l + 1))
                if l:
                    dve.wait_ge(s["ln2_done"], TB * l)
                for t in range(TB):
                    dve.wait_ge(s["mix_made"], TB * l + t + 1)
                    bank = pb[2 * t:2 * t + 2]
                    layer_norm(t, bank, mods[:, GT1, :], h, mods[:, SC2, :], mods[:, SH2, :], s["h2_ready"])

                def picks(g, t, part):
                    chain.sync()
                    if part == 0:
                        hold(dve, s["s_out"], g + (GROUPS * l + 1))
                        for q in range(2):
                            chain(v.max(top[:, q, 0:8], sc[:, t, q, :]))
                        chain.sync()
                        for q in range(2):
                            chain(v.max_index(topi[:, q, 0:8], top[:, q, 0:8], sc[:, t, q, :]))
                    elif part == 1:
                        for q in range(2):
                            chain(v.match_replace(sc[:, t, q, :], top[:, q, 0:8], sc[:, t, q, :], LOWEST))
                        chain.sync()
                        for q in range(2):
                            chain(v.max(top[:, q, 8:16], sc[:, t, q, :]))
                    elif part == 2:
                        for q in range(2):
                            chain(v.max_index(topi[:, q, 8:16], top[:, q, 8:16], sc[:, t, q, :]))
                        pairs(cand, top)
                        chain.sync()
                        chain(v.tensor_copy(topf[:, :, :], topi[:, :, :]))
                        chain(v.max(best[:, t, 0:8], cand[:, :]))
                    elif part == 3:
                        chain(v.tensor_scalar(topf[:, 0, :], topf[:, 0, :], float(NSUB), float(NEXP * l),
                                              ALU.mult, ALU.add))
                        chain(v.max_index(pos[:, 0:8], best[:, t, 0:8], cand[:, :]))
                        chain.sync()
                        chain(v.match_replace(cand[:, :], best[:, t, 0:8], cand[:, :], LOWEST))
                        pairs(cide, topf)
                    elif part == 4:
                        chain(v.max(best[:, t, 8:16], cand[:, :]))
                        chain.sync()
                        chain(v.max_index(pos[:, 8:16], best[:, t, 8:16], cand[:, :]))
                        v.tensor_scalar(nbest[:, t:t + 1], best[:, t, 0:1], -1.0, None, ALU.mult
                                        ).then_inc(s["picks_ready"], 1)
                        chain.sync()
                        chain(v.tensor_copy(posf[:, :], pos[:, :]))
                    elif part < 7:
                        lo = (part - 5) * (TOPK // 2)
                        cut = slice(lo, lo + TOPK // 2)
                        chain(v.tensor_tensor(eq, each(posf[:, cut], NCAND), over(iota_row, TOPK // 2), ALU.is_equal))
                        chain.sync()
                        chain(v.tensor_tensor(eq, eq, over(cide[:, :], TOPK // 2), ALU.mult))
                        chain.sync()
                        chain(v.tensor_reduce(eidf[:, cut], eq, AX.X, ALU.add))
                    else:
                        v.tensor_copy(uidx[:, t, :], eidf[:, :]).then_inc(s["idx_ready"], 1)

                def pairs(to, of):
                    lo = 0
                    for a, na, nb in RECTS:
                        chain(v.tensor_tensor(rows(to[:, lo:lo + na * nb], P, na), each(of[:, 0, a:a + na], nb),
                                              over(of[:, 1, 0:nb], na), ALU.add))
                        lo += na * nb

                def product(g, t, k):
                    uses = TOPK // UR
                    hold(dve, u_in[k % UR], (g * uses) * 16 + 16 * (GROUPS * uses * l + k // UR + 1))
                    v.scalar_tensor_tensor(ring[:, k % UR, :], ring[:, k % UR, :], 1.0, h[:, t, :], ALU.mult,
                                           ALU.mult, accum_out=dots[:, t, k:k + 1]).then_inc(s["u_used"], 1)

                def coefficients(g, t):
                    hold(dve, s["gate_out"], g + (GROUPS * l + 1))
                    chain(v.reciprocal(ginv[:, t:t + 1], gsum[:, t:t + 1]))
                    hold(dve, s["gelu_out"], g + (GROUPS * l + 1))
                    chain.sync()
                    v.scalar_tensor_tensor(coef[:, t, :], gel[:, t, :], ginv[:, t:t + 1], gexp[:, t, :],
                                           ALU.mult, ALU.mult).then_inc(s["coef_ready"], 1)

                def body(it, i, j, last):
                    t = (j + 1) % TB
                    if not (last and j + 1 >= SPAN):
                        for k in range(TOPK):
                            product(i + 1, t, k)
                            if k == 4:
                                hold(dve, s["v_used"], i * TOPK + (V_TURN * l + VR))
                                hold(dve, s["idx_ready"], i + (GROUPS * l + 2))
                                v.tensor_copy(vidx[:, t, :], uidx[:, t, :]).then_inc(s["vidx_ready"], 1)
                            if k < PICK_PARTS and not (last and j + 2 >= SPAN):
                                picks(i + 2, j % TB, k)
                        coefficients(i + 1, t)

                dve.wait_ge(s["h2_ready"], TB * (l + 1))
                for part in range(PICK_PARTS):
                    picks(0, 0, part)
                dve.sem_inc(s["u_used"], UR)
                dve.wait_ge(s["idx_ready"], GROUPS * l + 1)
                v.tensor_copy(vidx[:, 0, :], uidx[:, 0, :]).then_inc(s["vidx_ready"], 1)
                for k in range(TOPK):
                    product(0, 0, k)
                    if k < PICK_PARTS:
                        picks(1, 1, k)
                coefficients(0, 0)
                retrieval_loop(dve, body, chain, DVE_STEPS)
                dve.wait_ge(s["ln2_in"], 32 * (l + 1))
                dve.wait_ge(s["ln1_done"], TB * (l + 1))
                if l + 1 < LAYERS:
                    dve.wait_ge(s["ada_out"], 2 + GROUPS * (l + 1) + -(-2 * D // ADA_N))
                    fold(SC1, SH1, ln2[:, 0, :], ln2[:, 1, :], h[:, 1, :])
                for t in range(TB):
                    dve.wait_ge(s["y_made"], TB * l + t + 1)
                    if l + 1 < LAYERS:
                        layer_norm(t, Y[t], gt2, h, mods[:, SC1, :], mods[:, SH1, :], s["h_ready"])
                    else:
                        layer_norm(t, Y[t], gt2, xs, ln2[:, 0, :], ln2[:, 1, :], s["ln2_done"])

        @block.tensor
        def _(pe):
            mm = nc.tensor.matmul
            tr = nc.tensor.transpose

            def ada(l, i, j, turn, ks):
                to = ADA_BANK[j % 2][:, 0:ADA_N]
                if ks[0] == 0:
                    hold(pe, s[f"ada_in{j % 2}"], turn)
                    hold(pe, s["ada_out"], i + (GROUPS * l + 1))
                    mm(to, ones_row, brow[0:1, j % 2, :], start=True, stop=False)
                for k in ks:
                    e = mm(to, csb[:, k, :], ada_w[j % 2][:, k, :], start=False, stop=k == KC - 1)
                if ks[-1] == KC - 1:
                    e.then_inc(s["ada_made"], 1)

            pe.wait_ge(s["consts_in"], 16)
            pe.wait_ge(s["csb_ready"], 1)
            with pe.Fori(0, GROUPS // 2) as it:
                for j in range(2):
                    ada(0, it * 2 + j, j, it * 32 + 32, range(ADA_PE))
                    hold(pe, s["terms_ready"], it * 2 + (j + 1))
                    mm(ADA_BANK[j % 2][:, 0:ADA_N], ones_block, h[:, j % 2, 0:ADA_N], start=False, stop=True
                       ).then_inc(s["ada_made"], 1)

            for l in range(LAYERS):
                for b in range(4):
                    t, half = b // 2, b % 2
                    pe.wait_ge(s["h_ready"], TB * l + t + 1)
                    for k in range(4):
                        kk = 4 * half + k
                        e = tr(pb[b][:, k * P:(k + 1) * P], h[:, t, kk * P:(kk + 1) * P], ident)
                    e.then_inc(s["hT_made"], 1)
                pe.wait_ge(s["win_in"], 16 * (l + 1))
                pe.wait_ge(s["ada_out"], 2 + GROUPS * (l + 1))
                for b in range(6):
                    t, n = b // 3, b % 3
                    pe.wait_ge(s["hT_out"], 4 * l + 2 * (t + 1) if b < 4 else 4 * (l + 1))
                    to = pb[(4 + b) % 8 if b < 4 else b - 4][:, 0:PROJ_N]
                    for k in range(KC):
                        e = mm(to, hT[:, k, t * P:(t + 1) * P], win_w[:, k, n * PROJ_N:(n + 1) * PROJ_N],
                               start=k == 0, stop=k == KC - 1)
                    e.then_inc(s["proj_made"], 1)
                for t in range(TB):
                    pe.wait_ge(s["proj_out"], 6 * l + (3 if t == 0 else 6))
                    if t == 0:
                        pe.wait_ge(s["proj_out"], 6 * l + 3)
                    for a in range(SH):
                        e = tr(pb[4 + 2 * t][0:SD, a * P:(a + 1) * P], proj[:, t, O_QS + a * SD:O_QS + (a + 1) * SD], ident)
                    e.then_inc(s["sw_made"], 1)
                    for a in range(SKV):
                        e = tr(pb[5 + 2 * t][0:SD, a * P:(a + 1) * P], proj[:, t, O_KS + a * SD:O_KS + (a + 1) * SD], ident)
                    e.then_inc(s["sw_made"], 1)
                for t in range(TB):
                    pe.wait_ge(s["rms_ready"], TB * l + t + 1)
                    for n in range(3):
                        e = tr(pb[2 + t][:, n * P:(n + 1) * P], proj[:, t, n * P:(n + 1) * P], ident)
                    e.then_inc(s["cn_made"], 1)
                pe.wait_ge(s["glu_ready"], l + 1)
                for n in range(CC):
                    for t in range(TB):
                        e = tr(pb[0][:, (TB * n + t) * P:(TB * n + t + 1) * P],
                               proj[:, t, O_CONV + n * P:O_CONV + (n + 1) * P], ident)
                e.then_inc(s["conv_in_made"], 1)
                pe.wait_ge(s["wdr_in"], 16 * (l + 1))
                for n in range(CC):
                    e = tr(pb[1][:, n * P:n * P + TAPS], wdraw[0:TAPS, n * P:(n + 1) * P], ident[0:TAPS, 0:TAPS])
                e.then_inc(s["wd_made"], 1)
                pe.wait_ge(s["small_in"], 16 * SMALL_LOADS * (l + 1))
                pe.wait_ge(s["sw_out"], 4 * (l + 1))
                for t in range(TB):
                    bank = pb[4:8] if t == 0 else pb[0:4]
                    cut = slice(t * P, (t + 1) * P)
                    pe.wait_ge(s["cn_out"], TB * l + (1 if t == 0 else TB))
                    if t:
                        pe.wait_ge(s["wd_out"], l + 1)
                    for n in range(2):
                        for k in range(2):
                            e = mm(bank[n][:, 0:4 * QK], cqT[:, k, cut], wuq[:, k, n * 4 * QK:(n + 1) * 4 * QK],
                                   start=k == 0, stop=k == 1)
                        e.then_inc(s["qkv_made"], 1)
                    for n in range(2):
                        mm(bank[2 + n][:, :], ckvT[:, cut], wukv[:, n * 512:(n + 1) * 512], start=True, stop=True
                           ).then_inc(s["qkv_made"], 1)
                for t in range(TB):
                    bank = pb[4:8] if t == 0 else pb[0:4]
                    pe.wait_ge(s["qkv_out"], 12 * l + 6 * (t + 1))
                    pe.wait_ge(s["rope_ready"], TB * l + t + 1)
                    for n in range(4):
                        src = (qrows, krows)[n // 2][t]
                        for a in range(4):
                            e = tr(bank[n][0:QK, a * P:(a + 1) * P], src[:, 4 * (n % 2) + a, :], ident)
                        e.then_inc(s["hq_made"], 1)

                def scores(t, a, to):
                    n = P if t == 0 else 2 * P
                    q_, k_, w = (qTh[0:QK, a], kTh[0:QK, a], QK) if a < MH else \
                        (qsT[0:SD, a - MH], ksT[0:SD, (a - MH) // 2], SD)
                    return mm(to, q_[:, t * P:(t + 1) * P], k_[:, 0:n], start=True, stop=True)

                pe.wait_ge(s["hq_out"], 8 * (l + 1))
                for n in range(3):
                    for a in range(4):
                        e = scores(0, 4 * n + a, pb[n][:, a * P:(a + 1) * P])
                    e.then_inc(s["sc_made"], 1)
                for n in range(5):
                    for a in range(2):
                        e = scores(1, 2 * n + a, pb[3 + n][:, a * 2 * P:(a + 1) * 2 * P])
                    e.then_inc(s["sc_made"], 1)
                pe.wait_ge(s["exp_out"], TB * l + 1)
                pe.wait_ge(s["mask_out"], 9 * l + 3)
                for n in range(3):
                    for a in range(4):
                        e = tr(pb[n][:, a * P:(a + 1) * P], S[:, 4 * n + a, P:2 * P], ident)
                    e.then_inc(s["pT_made"], 1)

                def outputs(t):
                    for a in range(AH):
                        to = pb[0][:, a * MV:(a + 1) * MV] if a < MH else pb[1][:, (a - MH) * SD:(a - MH + 1) * SD]
                        for kb in range(0 if t else 1, 2):
                            blk = t if kb else 0
                            val = vrows[blk][:, a, :] if a < MH else \
                                proj[:, blk, O_VS + (a - MH) // 2 * SD:O_VS + ((a - MH) // 2 + 1) * SD]
                            e = mm(to, pT[:, a, kb, :], val, start=kb == 0 or t == 0, stop=kb == 1)
                    e.then_inc(s["o_made"], 1)

                pe.wait_ge(s["pT_out"], 9 * l + 3)
                outputs(0)
                for a in range(2):
                    e = scores(1, 10 + a, pb[2][:, a * 2 * P:(a + 1) * 2 * P])
                e.then_inc(s["sc_made"], 1)
                pe.wait_ge(s["exp_out"], TB * (l + 1))
                for n in range(6):
                    to = pb[3 + n] if n < 5 else pb[2]
                    for a in range(2):
                        for kb in range(2):
                            e = tr(to[:, (2 * a + kb) * P:(2 * a + kb + 1) * P], S[:, 2 * n + a, kb * P:(kb + 1) * P], ident)
                    e.then_inc(s["pT_made"], 1)
                pe.wait_ge(s["pT_out"], 9 * (l + 1))
                pe.wait_ge(s["o_out"], TB * l + 1)
                outputs(1)
                pe.wait_ge(s["o_out"], TB * (l + 1))
                for t in range(TB):
                    for n in range(CC):
                        e = tr(pb[7][:, t * CONV + n * P:t * CONV + (n + 1) * P], cacc[:, n, t * P:(t + 1) * P], ident)
                e.then_inc(s["conv_row_made"], 1)
                for t in range(TB):
                    for n in range(6):
                        to = pb[3 + 2 * t] if n < 4 else pb[4 + 2 * t]
                        e = tr(to[:, (n % 4) * P:(n % 4 + 1) * P], orow[:, t, n * P:(n + 1) * P], ident)
                        if n in (3, 5):
                            e.then_inc(s["oT_made"], 1)
                pe.wait_ge(s["conv_norm"], l + 1)
                for n in range(CC):
                    for t in range(TB):
                        e = tr(pb[2][:, (TB * n + t) * P:(TB * n + t + 1) * P], crow[:, t, n * P:(n + 1) * P], ident)
                e.then_inc(s["conv_col_made"], 1)
                pe.wait_ge(s["conv_act"], l + 1)
                for n in range(CC):
                    for k in range(CC):
                        e = mm(pb[7][:, n * SEQ:(n + 1) * SEQ], wpw[:, k, n * P:(n + 1) * P], hnT[:, k, :],
                               start=k == 0, stop=k == CC - 1)
                e.then_inc(s["conv_pw_made"], 1)
                pe.wait_ge(s["wo_in"], 16 * (l + 1))
                pe.wait_ge(s["oT_out"], 4 * (l + 1))
                pe.wait_ge(s["conv_pw_out"], l + 1)
                for t in range(TB):
                    bank = pb[2 * t:2 * t + 2]
                    for n in range(2):
                        for k in range(KC):
                            e = mm(bank[n][:, :], oT[:, k, t * P:(t + 1) * P], wo_w[:, k, n * 512:(n + 1) * 512],
                                   start=k == 0, stop=k == KC - 1)
                    e.then_inc(s["mix_made"], 1)
                pe.wait_ge(s["skr_in"], 16 * (l + 1))
                for b in range(4):
                    for k in range(4):
                        e = tr(pb[4 + b][:, k * P:(k + 1) * P], sk_raw[:, 4 * b + k, :], ident)
                    e.then_inc(s["sk_made"], 1)
                pe.wait_ge(s["sk_out"], 4 * (l + 1))

                def query_products(g, t, slot, turn, ks):
                    if ks[0] == 0:
                        hold(pe, s[f"wpq_in{slot}"], turn)
                        if not (isinstance(g, int) and g == 0):
                            hold(pe, s["s_out"], g + GROUPS * l)
                    for k in ks:
                        e = mm(Q_BANK[:, 0:2 * PK], hT[:, k, t * P:(t + 1) * P], wpq_w[slot][:, k, :],
                               start=k == 0, stop=k == KC - 1)
                    if ks[-1] == KC - 1:
                        e.then_inc(s["q_made"], 1)

                def query_transposes(g):
                    hold(pe, s["q_out"], g + (GROUPS * l + 1))
                    for q in range(2):
                        e = tr(QS_BANK[:, q * P:(q + 1) * P], qrow[:, q * PK:(q + 1) * PK], ident)
                    e.then_inc(s["qT_made"], 1)

                def query_scores(g, head):
                    hold(pe, s["qT_out"], g + (GROUPS * l + 1))
                    for q in range(2):
                        keys = skT[:, bass.ds(head * 2 + q, 1), :].rearrange("p a n -> p (a n)")
                        e = mm(QS_BANK[:, (2 + q) * P:(3 + q) * P], qT2[:, q, :], keys, start=True, stop=True)
                    e.then_inc(s["s_made"], 1)

                def weigh(i, t, k):
                    uses = TOPK // VR
                    hold(pe, v_in[k % VR], (i * uses) * 16 + 16 * (GROUPS * uses * l + k // VR + 1))
                    hold(pe, s["diag_ready"], i * TOPK + (PICKS * l + k + 1))
                    for n in range(2):
                        e = mm(Y[t][n][:, :], diag[:, k % VR, :], ring[:, UR + k % VR, n * 512:(n + 1) * 512],
                               start=False, stop=False)
                    e.then_inc(s["v_used"], 1)

                def body(it, i, j, last):
                    t = j % TB
                    asks = not (last and j + 3 >= SPAN)
                    hd = (j + 3) // TB
                    for k in range(TOPK):
                        if asks and 4 <= k < 8:
                            query_products(i + 3, (j + 3) % TB, hd % 2,
                                           it * 16 + 16 * (PH // 2 * l + (j + 3) // SPAN + 1),
                                           range(2 * k - 8, 2 * k - 6))
                        weigh(i, t, k)
                        if asks and k == 8:
                            query_transposes(i + 3)
                        if asks and k == 9:
                            query_scores(i + 3, it * (SPAN // TB) + hd)
                        if l + 1 < LAYERS and k in (10, 11, 12):
                            ada(l + 1, i, j, it * (SPAN // 2 * 32) + 32 * (GROUPS // 2 * (l + 1) + j // 2 + 1),
                                range((0, 3, 6)[k - 10], (3, 6, KC)[k - 10]))
                    if last and j >= SPAN - TB:
                        for n in range(2):
                            e = mm(Y[t][n][:, :], zero_row, any_row, start=False, stop=True)
                        e.then_inc(s["y_made"], 1)

                for g in range(3):
                    t = g % TB
                    if g < TB:
                        pe.wait_ge(s["h2_ready"], TB * l + t + 1)
                        for half in range(2):
                            for k in range(4):
                                kk = 4 * half + k
                                e = tr(pb[2 * t + half][:, k * P:(k + 1) * P], h[:, t, kk * P:(kk + 1) * P], ident)
                            e.then_inc(s["h2T_made"], 1)
                        pe.wait_ge(s["h2T_out"], 4 * l + 2 * (t + 1))
                    query_products(g, t, (g // TB) % 2, 16 * (PH // 2 * l + 1), range(KC))
                    query_transposes(g)
                    query_scores(g, g // TB)
                for t in range(TB):
                    for n in range(2):
                        e = mm(Y[t][n][:, :], zero_row, any_row, start=True, stop=False)
                pe.sem_inc(s["v_used"], VR)
                retrieval_loop(pe, body)


def shape_constants(np):
    k = np.zeros((P, C_END), np.float32)
    i, j = np.arange(P)[:, None], np.arange(P)[None, :]
    k[:, C_ID:C_ID + P] = i == j
    own = np.where(j <= i, 0.0, MASKED)
    k[:, C_FULL + P:C_FULL + 2 * P] = own
    k[:, C_BAND:C_BAND + P] = np.where(j > i, 0.0, MASKED)
    k[:, C_BAND + P:C_BAND + 2 * P] = own
    half = ROPE // 2
    inv = (1.0 / (np.float32(10000.0) ** (np.arange(0, ROPE, 2, dtype=np.float32) / np.float32(ROPE)))).astype(np.float32)
    for t in range(TB):
        ang = (np.arange(t * P, (t + 1) * P, dtype=np.float32)[:, None] * inv[None, :]).astype(np.float32)
        k[:, C_COS + t * half:C_COS + (t + 1) * half] = np.cos(ang)
        k[:, C_SIN + t * half:C_SIN + (t + 1) * half] = np.sin(ang)
    k[:, C_IOTA:C_IOTA + NCAND] = np.arange(NCAND)
    k[:, C_ONES:C_ONES + P] = 1.0
    k[:, C_HALF:C_HALF + 2] = -0.5
    return k


_INS = ["x", "c", "w_ada", "b_ada", "w_in", "g_q", "w_uq", "g_kv", "w_ukv", "w_dw", "b_dw", "g_conv", "b_conv",
        "w_pw", "b_pw", "sinks", "w_o", "g_ln1", "b_ln1", "w_pq", "sub_keys", "u_tab", "v_tab", "g_ln2", "b_ln2"]


def kernel(**inputs):
    import numpy as _np
    import concourse.bacc as _bacc
    from concourse import mybir as _mybir
    from concourse.bass_utils import run_bass_kernel_spmd as _run

    nc = _bacc.Bacc("TRN2", target_bir_lowering=False, num_devices=1)
    arrays, args = {}, []
    for name in _INS:
        a = _np.ascontiguousarray(inputs[name])
        arrays[f"in_{name}"] = a
        args.append(nc.dram_tensor(f"in_{name}", a.shape, _mybir.dt.from_np(a.dtype), kind="ExternalInput").ap())
    k = shape_constants(_np)
    arrays["in_consts"] = k
    args.append(nc.dram_tensor("in_consts", k.shape, _mybir.dt.float32, kind="ExternalInput").ap())
    args.append(nc.dram_tensor("out_0", (1, SEQ, D), _mybir.dt.float32, kind="ExternalOutput").ap())
    build(nc, *args)
    r = _run(nc, [arrays], core_ids=[0])
    return r.results[0]["out_0"]
```

```python
import concourse.bass as bass
from concourse import mybir
from concourse.alu_op_type import AluOpType as ALU
from contextlib import ExitStack

F32 = mybir.dt.float32
U32 = mybir.dt.uint32
ACT = mybir.ActivationFunctionType
AX = mybir.AxisListType

P = 128
LAYERS = 2
D = 1024
SEQ = 256
TB = SEQ // P
KC = D // P
Q_RANK, KV_RANK, ROPE, CONV, TAPS = 256, 128, 32, 256, 31
MH, NOPE, MV = 8, 64, 64
QK = NOPE + ROPE
SH, SKV, SD = 4, 2, 64
AH = MH + SH
O_CQ, O_CKV, O_KR, O_CONV = 0, 256, 384, 416
O_QS, O_KS, O_VS = 928, 1184, 1312
D_IN = 1440
PROJ_N = D_IN // 3
CC = CONV // P
PAD = TAPS - 1
PH, PK, TOPK, NSUB = 8, 128, 16, 128
NEXP = NSUB * NSUB
GROUPS = PH * TB
ADA_N = 6 * D // GROUPS
ALPHA = float((2 * LAYERS) ** 0.25)
EPS = 1e-6
MLA_SCALE = float(QK) ** -0.5
SWA_SCALE = float(SD) ** -0.5
LOWEST = -3.0e38
MASKED = -1.0e30
SH1, SC1, GT1, SH2, SC2, GT2 = range(6)

RECTS = [(0, 1, 16), (1, 1, 8), (2, 2, 5), (4, 4, 3), (8, 8, 1)]
NCAND = sum(na * nb for _, na, nb in RECTS)

C_ID = 0
C_FULL = C_ID + P
C_BAND = C_FULL + 2 * P
C_COS = C_BAND + 2 * P
C_SIN = C_COS + TB * ROPE // 2
C_IOTA = C_SIN + TB * ROPE // 2
C_ONES = C_IOTA + NCAND
C_HALF = C_ONES + P
C_END = C_HALF + 2

UR = 4
VR = 4
SPAN = 4
PICKS = GROUPS * TOPK
U_TURN = PICKS + UR
V_TURN = PICKS + VR
DVE_STEPS = 35
PICK_PARTS = 8
SMALL_LOADS = 10
ADA_C = ADA_N // P
ADA_FIRST = 6
COLS_B = 6 * KC
GT1_ROW, SC2_ROW, SH2_ROW, GT2_ROW = range(4)
TICK = [None]


def hold(eng, sem, value):
    eng.wait_ge(sem, value)
    if not isinstance(value, int):
        eng.sem_inc(TICK[0], 1)


class Chain:

    def __init__(self, eng, sem):
        self.eng, self.sem, self.base, self.n = eng, sem, 0, 0

    def __call__(self, ins):
        ins.then_inc(self.sem, 1)
        self.n += 1

    def sync(self):
        hold(self.eng, self.sem, self.base + self.n)


def retrieval_loop(eng, body, chain=None, steps=0):
    spans = GROUPS // SPAN
    start = chain.base + chain.n if chain else 0
    with eng.Fori(0, spans - 1) as it:
        for j in range(SPAN):
            if chain:
                chain.base, chain.n = it * (SPAN * steps) + (start + j * steps), 0
            body(it, it * SPAN + j, j, False)
            if chain:
                assert chain.n == steps, chain.n
    if chain:
        chain.base, chain.n = start + (spans - 1) * SPAN * steps, 0
    for j in range(SPAN):
        body(spans - 1, (spans - 1) * SPAN + j, j, True)


def build(nc, x, c, w_ada, b_ada, w_in, g_q, w_uq, g_kv, w_ukv, w_dw, b_dw, g_conv, b_conv, w_pw,
          b_pw, sinks, w_o, g_ln1, b_ln1, w_pq, sub_keys, u_tab, v_tab, g_ln2, b_ln2, consts, out):
    ctx = ExitStack()
    with ctx:
        def sb(name, shape, dt=F32):
            return ctx.enter_context(nc.sbuf_tensor(name, shape, dt))

        cst = sb("cst", [P, C_END])
        win = sb("win", [P, KC * D_IN])
        ring = sb("ring", [P, UR + VR, D])
        wo = sb("wo", [P, KC * D])
        wpq = sb("wpq", [P, 2, KC * 2 * PK])
        mods = sb("mods", [P, 4, D])
        modc = sb("modc", [P, LAYERS, COLS_B])
        colT = sb("colT", [P, LAYERS * (COLS_B + 4 * KC)])
        lift = sb("lift", [P, KC])
        lnr3 = sb("lnr3", [P, 3, D])
        xs = sb("xs", [P, TB, D])
        h = sb("h", [P, TB, D])
        hT = sb("hT", [P, KC, SEQ])
        skT = sb("skT", [P, 2 * PH, NSUB])
        ccol = sb("ccol", [P, KC])
        cols = sb("cols", [P, 12])
        sinkb = sb("sinkb", [P, SH])
        sinkd = sb("sinkd", [P, SH])
        wdT = sb("wdT", [P, CC, TAPS])
        stat = sb("stat", [P, 16])
        krot = sb("krot", [P, 4, ROPE // 2])
        rowmax = sb("rowmax", [P, AH])
        nmax = sb("nmax", [P, AH])
        rsum = sb("rsum", [P, AH])
        rinv = sb("rinv", [P, TB, AH])
        qrow = sb("qrow", [P, 2 * PK])
        qT2 = sb("qT2", [P, 2, P])
        sc = sb("sc", [P, TB, 2, NSUB])
        top = sb("top", [P, 2, TOPK])
        topi = sb("topi", [P, 2, TOPK], U32)
        topf = sb("topf", [P, 2, TOPK])
        cand = sb("cand", [P, NCAND])
        cide = sb("cide", [P, NCAND])
        pos = sb("pos", [P, TOPK], U32)
        posf = sb("posf", [P, TOPK])
        junk = sb("junk", [P, 512])
        eidf = sb("eidf", [P, TOPK])
        best = sb("best", [P, TB, TOPK])
        nbest = sb("nbest", [P, TB])
        warm = sb("warm", [P, TB])
        uidx = sb("uidx", [P, TB, TOPK], U32)
        vidx = sb("vidx", [P, TB, TOPK], U32)
        gexp = sb("gexp", [P, TB, TOPK])
        gsum = sb("gsum", [P, TB])
        ginv = sb("ginv", [P, TB])
        dots = sb("dots", [P, TB, TOPK])
        gel = sb("gel", [P, TB, TOPK])
        coef = sb("coef", [P, TB, TOPK])
        diag = sb("diag", [P, VR, P])

        ident = cst[:, C_ID:C_ID + P]
        full_mask = cst[:, C_FULL:C_FULL + 2 * P]
        band_mask = cst[:, C_BAND:C_BAND + 2 * P]
        own_mask = cst[:, C_FULL + P:C_FULL + 2 * P]
        ones_row = cst[0:1, C_ONES:C_ONES + P]
        ones_col = cst[:, C_ONES:C_ONES + 1]
        zero_row = cst[0:1, C_FULL:C_FULL + P]
        any_row = cst[0:1, 0:512]
        iota_row = cst[:, C_IOTA:C_IOTA + NCAND]

        def view(t, lo, *shape):
            n = 1
            for d in shape:
                n *= d
            ap = t[:, lo:lo + n]
            if len(shape) == 2:
                return ap.rearrange("p (a b) -> p a b", a=shape[0])
            if len(shape) == 3:
                return ap.rearrange("p (a b c) -> p a b c", a=shape[0], b=shape[1])
            return ap

        def rows(ap, parts, shape):
            return ap[0:parts].rearrange("p (a b) -> p a b", a=shape)

        def over(ap, n):
            return ap.unsqueeze(1).to_broadcast([P, n, ap.shape[1]])

        def each(ap, n):
            return ap.unsqueeze(2).to_broadcast([P, ap.shape[1], n])

        win_w = view(win, 0, KC, D_IN)
        wo_w = view(wo, 0, KC, D)
        lnr = lnr3[:, 0:2, :]
        ada_w = [view(wo, t * KC * ADA_N, KC, ADA_N) for t in range(2)]
        wpq_w = [wpq[:, t, :].rearrange("p (k n) -> p k n", k=KC) for t in range(2)]
        small = wpq[:, :, :].rearrange("p s n -> p (s n)")
        wuq = view(small, 0, 2, MH * QK)
        wukv = view(small, 1536, MH * (NOPE + MV))
        wpw = view(small, 2560, CC, CONV)
        rr = ring[:, :, :].rearrange("p s n -> p (s n)")
        proj = view(rr, 0, TB, D_IN)
        qrows = [view(rr, 2880 + t * MH * QK, MH, QK) for t in range(TB)]
        krows = [view(rr, 4416 + t * MH * QK, MH, QK) for t in range(TB)]
        vrows = [view(rr, 5952 + t * MH * MV, MH, MV) for t in range(TB)]
        pT = view(rr, 2880, AH, 2, P)
        raw_b, raw_ln = skT[0:LAYERS * COLS_B, 0, :], skT[0:4 * LAYERS * KC, 1, :]
        qTh = view(win, 0, MH, SEQ)
        kTh = view(win, 2048, MH, SEQ)
        qsT = view(win, 4096, SH, SEQ)
        ksT = view(win, 5120, SKV, SEQ)
        S = view(win, 5632, AH, 2 * P)
        hc = view(win, 8704, CC, PAD + SEQ)
        cacc = view(win, 9276, CC, SEQ)
        crow = view(win, 9788, TB, CONV)
        cqT = view(win, 10300, 2, SEQ)
        ckvT = view(win, 10812, SEQ)
        wdraw = view(win, 11068, CONV)
        orow, oT = h, hT
        hnT = cacc
        sk_raw = view(win, 0, 2 * PH, PK)
        eq = view(junk, 0, TOPK // 2, NCAND)

        pb = [ctx.enter_context(nc.psum_tensor(f"pb{i}", [P, 512], F32)) for i in range(8)]
        Y = [(pb[0], pb[1]), (pb[2], pb[3])]
        Q_BANK, QS_BANK, ADA_BANK = pb[4], pb[5], (pb[6], pb[7])

        def mcol(l, part, k):
            return modc[:, l, part * KC + k:part * KC + k + 1]

        sum_batches = [(range(ADA_FIRST), pb[6]), (range(6, 12), pb[2]), (range(12, 13), pb[7]), (range(13, 16), pb[0])]
        sums_behind_projection = {1: (6,), 2: (7,), 3: (8,), 4: (9,), 5: (10, 11)}
        sums_behind_qkv, sums_behind_scores = (12,), (13, 14, 15)
        POOL_CHUNKS, POOL_BATCH = 6, 4
        IN_SPAN = POOL_CHUNKS + 1

        def in_span(j):
            left, groups = GROUPS - IN_SPAN, SPAN - 1
            return range(IN_SPAN + left * j // groups, IN_SPAN + left * (j + 1) // groups) if j < groups else range(0)

        def ada_tile(i):
            lo = KC * ADA_N
            return (view(win, 0, KC, ADA_N), view(win, lo, KC, ADA_N), view(win, 2 * lo, KC, ADA_N),
                    view(rr, 0, KC, ADA_N), view(rr, lo, KC, ADA_N))[i] if i < 5 else ada_w[i % 2]

        def pool_tile(i):
            tiles = (view(lnr3[:, :, :].rearrange("p a n -> p (a n)"), 0, KC, ADA_N), ada_w[0], ada_w[1])
            return tiles[(0, 0, 0, 1, 2, 0)[i]]

        def pool_place(i):
            if i < POOL_BATCH:
                return mods[:, :, :].rearrange("p a n -> p (a n)")[:, i * ADA_N:(i + 1) * ADA_N]
            return view(rr, 6976 + (i - POOL_BATCH) * ADA_N, ADA_N)

        def terms_place(i):
            if i == 14:
                return view(rr, 6976 + 2 * ADA_N, ADA_N)
            return h[:, i % 2, (i // 2 % 2) * 512:(i // 2 % 2) * 512 + ADA_N]

        names = """tick dve_chain consts_in c_in x_in cs_ready rows_in cols_made cols_out cols_ready ada_in0 ada_in1 ada_made terms_ready pool_terms pool_chain pool_in0 pool_in1 pool_in2 pool_made pool_out late_in0 late_in1 late_made late_out
        ada_out xn_ready hTd_out hn_ready rep_made rep_out win_in small_in wo_in ln_in skr_in wdr_in hT_made hT_out proj_made
        proj_out sw_made sw_out rms_ready glu_sig glu_ready cn_made cn_out qkv_made qkv_out rope_ready
        hq_made hq_out conv_in_made conv_in_out wd_made wd_out conv_ready conv_row_made conv_norm
        conv_col_made conv_act conv_pw_made conv_pw_out sc_made mask_out max_ready exp_out pT_made
        pT_out o_made o_out oT_made oT_out mix_made ln1_done h2_ready h2T_made h2T_out sk_made sk_out
        gained var_ready root_out q_made q_out qT_made qT_out s_made s_out wpq_in0 wpq_in1 idx_ready picks_ready
        gate_out u_used gelu_out coef_ready vidx_ready diag_ready v_used y_made ln2_done
        out_stored""".split()
        s = {n: ctx.enter_context(nc.semaphore(n)) for n in names}
        TICK[0] = s["tick"]
        first_in = [ctx.enter_context(nc.semaphore(f"first_in{i}")) for i in range(ADA_FIRST)]
        u_in = [ctx.enter_context(nc.semaphore(f"u_in{i}")) for i in range(UR)]
        v_in = [ctx.enter_context(nc.semaphore(f"v_in{i}")) for i in range(VR)]

        block = ctx.enter_context(nc.Block())
        u_flat = u_tab.rearrange("l e d -> (l e) d")
        v_flat = v_tab.rearrange("l e d -> (l e) d")

        @block.sync
        def _(sp):
            sp.dma_start(cst[:, :], consts).then_inc(s["consts_in"], 16)
            sp.dma_start(ccol[:, :], c.rearrange("b (k p) -> p (b k)", p=P), allow_slow_non_contiguous=True).then_inc(s["c_in"], 16)

            def load_small(l):
                got = s["small_in"]
                sp.dma_start(wuq, w_uq[l].rearrange("(k p) n -> p k n", p=P)).then_inc(got, 16)
                sp.dma_start(wukv, w_ukv[l]).then_inc(got, 16)
                sp.dma_start(wpw, w_pw[l].rearrange("(k p) n -> p k n", p=P)).then_inc(got, 16)
                sp.dma_start(cols[:, 0:2], g_q[l].rearrange("(k p) -> p k", p=P), allow_slow_non_contiguous=True).then_inc(got, 16)
                sp.dma_start(cols[:, 2:3], g_kv[l].rearrange("(k p) -> p k", p=P), allow_slow_non_contiguous=True).then_inc(got, 16)
                for j, w in enumerate((b_dw, g_conv, b_conv, b_pw)):
                    sp.dma_start(cols[:, 3 + 2 * j:5 + 2 * j], w[l].rearrange("(k p) -> p k", p=P),
                                 allow_slow_non_contiguous=True).then_inc(got, 16)
                sp.dma_start(sinkb[:, :], sinks[l:l + 1, :].to_broadcast([P, SH])).then_inc(got, 16)

            def wpq_load(l, hd):
                src = w_pq[l].rearrange("(k p) n -> p k n", p=P)[:, :, hd * 2 * PK:(hd + 1) * 2 * PK]
                sp.dma_start(wpq_w[hd % 2], src).then_inc(s[f"wpq_in{hd % 2}"], 16)

            def ln_load(l, gain, offset):
                for j, w in enumerate((gain, offset)):
                    sp.dma_start(lnr[:, j, :], w[l:l + 1, :].to_broadcast([P, D])).then_inc(s["ln_in"], 16)

            sp.dma_start(raw_b, b_ada.rearrange("l (j p) -> (l j) p", p=P)).then_inc(s["rows_in"], 16)
            for j, w in enumerate((g_ln1, b_ln1, g_ln2, b_ln2)):
                n = LAYERS * KC
                sp.dma_start(raw_ln[j * n:(j + 1) * n, :], w.rearrange("l (k p) -> (l k) p", p=P)
                             ).then_inc(s["rows_in"], 16)
            def chunk_load(i):
                got = first_in[i] if i < ADA_FIRST else s[f"ada_in{i % 2}"]
                sp.dma_start(ada_tile(i), w_ada[0].rearrange("(k p) n -> p k n", p=P)[:, :, i * ADA_N:(i + 1) * ADA_N]
                             ).then_inc(got, 16)

            def next_load(i, to, got):
                sp.dma_start(to, w_ada[1].rearrange("(k p) n -> p k n", p=P)[:, :, i * ADA_N:(i + 1) * ADA_N]
                             ).then_inc(got, 16)

            def pool_load(i):
                next_load(i, pool_tile(i), s[f"pool_in{i % 3}"])

            for i in range(ADA_FIRST):
                chunk_load(i)
            sp.dma_start(xs[:, :, :], x[0].rearrange("(t p) d -> p t d", p=P)).then_inc(s["x_in"], 16)
            sp.wait_ge(s["terms_ready"], 3)
            sp.dma_start(win_w, w_in[0].rearrange("(k p) n -> p k n", p=P)).then_inc(s["win_in"], 16)
            for i in (ADA_FIRST, ADA_FIRST + 1):
                sp.wait_ge(s["terms_ready"], ADA_FIRST)
                chunk_load(i)
            for l in range(LAYERS):
                if l:
                    sp.wait_ge(s["s_made"], GROUPS * l)
                load_small(l)
                if l:
                    sp.wait_ge(s["late_made"], GROUPS - POOL_CHUNKS)
                    sp.wait_ge(s["y_made"], TB * l)
                    sp.dma_start(wo_w, w_o[l].rearrange("(k p) n -> p k n", p=P)).then_inc(s["wo_in"], 16)
                else:
                    for i in range(ADA_FIRST + 2, GROUPS - 2):
                        sp.wait_ge(s["terms_ready"], i - 1)
                        chunk_load(i)
                        if i == ADA_FIRST + 2:
                            pool_load(0)
                        if i == 13:
                            sp.wait_ge(s["pool_terms"], 1)
                            pool_load(1)
                sp.wait_ge(s["proj_made"], 3 * TB * (l + 1))
                sp.dma_start(wdraw[0:TAPS, :], w_dw[l]).then_inc(s["wdr_in"], 16)
                if l == 0:
                    for i in (GROUPS - 2, GROUPS - 1):
                        sp.wait_ge(s["terms_ready"], i - 1)
                        chunk_load(i)
                    for i in range(2, POOL_CHUNKS):
                        if i in (3, 4):
                            sp.wait_ge(s["terms_ready"], GROUPS - 4 + i)
                        else:
                            sp.wait_ge(s["pool_terms"], {2: 2, 5: 3}[i])
                        pool_load(i)
                    sp.wait_ge(s["pool_terms"], POOL_CHUNKS - 1)
                else:
                    sp.wait_ge(s["ln2_done"], TB * l)
                if l == 0:
                    sp.dma_start(wo_w, w_o[l].rearrange("(k p) n -> p k n", p=P)).then_inc(s["wo_in"], 16)
                if l == 0:
                    sp.wait_ge(s["pool_terms"], POOL_CHUNKS)
                ln_load(l, g_ln1, b_ln1)
                sp.wait_ge(s["sc_made"], 9 * (l + 1))
                sp.dma_start(sk_raw, sub_keys[l].rearrange("h q n d -> n (h q) d")).then_inc(s["skr_in"], 16)
                sp.wait_ge(s["conv_pw_made"], l + 1)
                for hd in range(2):
                    wpq_load(l, hd)
                sp.wait_ge(s["mix_made"], TB * (l + 1))
                ahead = l + 1 < LAYERS
                if ahead:
                    for i in range(POOL_CHUNKS, IN_SPAN):
                        next_load(i, ada_w[i % 2], s[f"late_in{i % 2}"])
                for hd in range(2, PH):
                    sp.wait_ge(s["q_made"], GROUPS * l + TB * (hd - 1))
                    wpq_load(l, hd)
                    if hd == 2:
                        sp.wait_ge(s["ln1_done"], TB * (l + 1))
                        ln_load(l, g_ln2, b_ln2)
                if ahead:
                    for i in range(IN_SPAN, GROUPS):
                        if i > POOL_CHUNKS + 1:
                            sp.wait_ge(s["late_made"], i - POOL_CHUNKS - 1)
                        next_load(i, ada_w[i % 2], s[f"late_in{i % 2}"])
                    sp.wait_ge(s["sk_made"], 4 * (l + 1))
                    sp.wait_ge(s["v_used"], V_TURN * (l + 1) - VR + 1)
                    sp.dma_start(win_w, w_in[l + 1].rearrange("(k p) n -> p k n", p=P)).then_inc(s["win_in"], 16)
            for t in range(TB):
                sp.wait_ge(s["ln2_done"], TB * (LAYERS - 1) + t + 1)
                sp.dma_start(out[0, t * P:(t + 1) * P, :], xs[:, t, :]).then_inc(s["out_stored"], 16)
            sp.wait_ge(s["out_stored"], 16 * TB)

        @block.gpsimd
        def _(pool):
            asked = gained = 0

            def reciprocal_roots(lo, n, times):
                nonlocal asked
                for _ in range(times):
                    asked += 1
                    pool.wait_ge(s["var_ready"], asked)
                    nc.gpsimd.tensor_tensor(stat[:, lo:lo + n], stat[:, lo:lo + n],
                                            cst[:, C_HALF:C_HALF + n], ALU.pow).then_inc(s["root_out"], 1)

            chained = 0

            def terms(i):
                nonlocal chained
                pool.wait_ge(s[f"pool_in{i % 3}"], 16 * (i // 3 + 1))
                w = pool_tile(i)
                half, quarter = KC // 2, KC // 4
                c_each = ccol[:, :].unsqueeze(2).to_broadcast([P, KC, ADA_N])
                for to, a_, b_, op in ((w, w, c_each, ALU.mult),
                                       (w[:, 0:half], w[:, 0:half], w[:, half:KC], ALU.add),
                                       (w[:, 0:quarter], w[:, 0:quarter], w[:, quarter:half], ALU.add)):
                    nc.gpsimd.tensor_tensor(to, a_, b_, op).then_inc(s["pool_chain"], 1)
                    chained += 1
                    pool.wait_ge(s["pool_chain"], chained)
                nc.gpsimd.tensor_tensor(pool_place(i), w[:, 0, :], w[:, 1, :], ALU.add).then_inc(s["pool_terms"], 1)

            def gain_and_offset(t, done):
                nonlocal gained
                nc.gpsimd.tensor_tensor(xs[:, t, :], xs[:, t, :], lnr[:, 0, :], ALU.mult).then_inc(s["gained"], 1)
                gained += 1
                pool.wait_ge(s["gained"], gained)
                nc.gpsimd.tensor_tensor(xs[:, t, :], xs[:, t, :], lnr[:, 1, :], ALU.add).then_inc(done, 1)

            for l in range(LAYERS):
                reciprocal_roots(0, 2, 1)
                if l == 0:
                    pool.wait_ge(s["cs_ready"], 1)
                    terms(0)
                reciprocal_roots(0, 2, 1)
                if l == 0:
                    for i in range(1, POOL_CHUNKS):
                        terms(i)
                reciprocal_roots(13, 1, TB)
                reciprocal_roots(13, 1, TB)
                pool.wait_ge(s["ln_in"], 64 * l + 32)
                for t in range(TB):
                    pool.wait_ge(s["h2_ready"], TB * l + t + 1)
                    pool.wait_ge(s["h2T_made"], 4 * l + 2 * (t + 1))
                    gain_and_offset(t, s["ln1_done"])

                def gather_u(i, t, k):
                    hold(pool, s["u_used"], i * TOPK + (U_TURN * l + k + 1))
                    nc.gpsimd.indirect_dma_start(
                        out=ring[:, k % UR, :], out_offset=None, in_=u_flat,
                        in_offset=bass.IndirectOffsetOnAxis(ap=uidx[:, t, k:k + 1], axis=0)
                    ).then_inc(u_in[k % UR], 16)

                def gather_v(i, t, k):
                    hold(pool, s["v_used"], i * TOPK + (V_TURN * l + k + 1))
                    nc.gpsimd.indirect_dma_start(
                        out=ring[:, UR + k % VR, :], out_offset=None, in_=v_flat,
                        in_offset=bass.IndirectOffsetOnAxis(ap=vidx[:, t, k:k + 1], axis=0)
                    ).then_inc(v_in[k % VR], 16)

                def body(it, i, j, last):
                    more = not (last and j == SPAN - 1)
                    if more:
                        hold(pool, s["idx_ready"], i + (GROUPS * l + 2))
                    hold(pool, s["vidx_ready"], i + (GROUPS * l + 1))
                    for k in range(TOPK):
                        if more:
                            gather_u(i + 1, (j + 1) % TB, k)
                        gather_v(i, j % TB, k)

                pool.wait_ge(s["idx_ready"], GROUPS * l + 1)
                for k in range(TOPK):
                    gather_u(0, 0, k)
                retrieval_loop(pool, body)
                reciprocal_roots(13, 1, TB)
                if l + 1 < LAYERS:
                    pool.wait_ge(s["ln_in"], 64 * (l + 1))
                    for t in range(TB):
                        pool.wait_ge(s["hT_made"], 4 * (l + 1) + 2 * (t + 1))
                        gain_and_offset(t, s["ln2_done"])

        @block.scalar
        def _(act):
            copy = nc.scalar.copy
            f = nc.scalar.activation

            def sums_out(n):
                chunks, bank = sum_batches[n]
                act.wait_ge(s["ada_made"], chunks[-1] + 1)
                lo, m = chunks[0] * ADA_C, len(chunks) * ADA_C
                copy(modc[:, 0, lo:lo + m], bank[:, 0:m]).then_inc(s["ada_out"], len(chunks))

            def pool_sums_out(n, bank):
                lo, hi = ((0, POOL_BATCH), (POOL_BATCH, POOL_CHUNKS))[n]
                act.wait_ge(s["pool_made"], n + 1)
                copy(modc[:, 1, lo * ADA_C:hi * ADA_C], bank[:, 0:(hi - lo) * ADA_C]).then_inc(s["pool_out"], 1)

            def late_out(i):
                act.wait_ge(s["late_made"], i - POOL_CHUNKS + 1)
                copy(modc[:, 1, i * ADA_C:(i + 1) * ADA_C], ADA_BANK[i % 2][:, 0:ADA_C]).then_inc(s["late_out"], 1)

            def rows_out(l, part, banks):
                act.wait_ge(s["rep_made"], 4 * l + part + 1)
                for n in range(2):
                    e = copy(mods[:, part, n * 512:(n + 1) * 512], banks[n][:, :])
                e.then_inc(s["rep_out"], 1)

            act.wait_ge(s["c_in"], 16)
            f(ccol[:, :], ccol[:, :], ACT.Silu).then_inc(s["cs_ready"], 1)
            act.wait_ge(s["cols_made"], 1)
            nb, nl = LAYERS * COLS_B, 4 * LAYERS * KC
            copy(colT[:, 0:nb], pb[0][:, 0:nb])
            copy(colT[:, nb:nb + nl], pb[1][:, 0:nl]).then_inc(s["cols_out"], 1)
            sums_out(0)

            for l in range(LAYERS):
                act.wait_ge(s["cols_ready"], 1 if l == 0 else l + 2)
                for t in range(TB):
                    act.wait_ge(s["hT_made"], 4 * l + 2 * t + 1)
                    for k in range(4):
                        e = f(hT[:, k, t * P:(t + 1) * P], pb[2 * t][:, k * P:(k + 1) * P], ACT.Identity,
                              scale=mcol(l, SC1, k), bias=mcol(l, SH1, k))
                    e.then_inc(s["hT_out"], 1)
                for b in range(6):
                    act.wait_ge(s["proj_made"], 6 * l + b + 1)
                    t, n = b // 3, b % 3
                    copy(proj[:, t, n * PROJ_N:(n + 1) * PROJ_N], pb[(4 + b) % 8 if b < 4 else b - 4][:, 0:PROJ_N]
                         ).then_inc(s["proj_out"], 1)
                if l == 0:
                    sums_out(1)
                act.wait_ge(s["proj_out"], 6 * (l + 1))
                gate = proj[:, :, O_CONV + CONV:O_CONV + 2 * CONV]
                f(gate, gate, ACT.Sigmoid).then_inc(s["glu_sig"], 1)
                act.wait_ge(s["small_in"], 16 * SMALL_LOADS * (l + 1))
                for t in range(TB):
                    cut = slice(t * P, (t + 1) * P)
                    act.wait_ge(s["sw_made"], 4 * l + 2 * t + 1)
                    copy(qsT[0:SD, :, cut], rows(pb[4 + 2 * t], SD, 4)).then_inc(s["sw_out"], 1)
                    act.wait_ge(s["sw_made"], 4 * l + 2 * t + 2)
                    copy(ksT[0:SD, :, cut], rows(pb[5 + 2 * t][:, 0:2 * P], SD, 2)).then_inc(s["sw_out"], 1)
                for t in range(TB):
                    cut = slice(t * P, (t + 1) * P)
                    act.wait_ge(s["cn_made"], TB * l + t + 1)
                    f(cqT[:, 0, cut], pb[2 + t][:, 0:P], ACT.Copy, scale=cols[:, 0:1])
                    f(cqT[:, 1, cut], pb[2 + t][:, P:2 * P], ACT.Copy, scale=cols[:, 1:2])
                    f(ckvT[:, cut], pb[2 + t][:, 2 * P:3 * P], ACT.Copy, scale=cols[:, 2:3]
                      ).then_inc(s["cn_out"], 1)
                act.wait_ge(s["conv_in_made"], l + 1)
                copy(hc[:, :, PAD:PAD + SEQ], rows(pb[0], P, 2)).then_inc(s["conv_in_out"], 1)
                act.wait_ge(s["wd_made"], l + 1)
                copy(wdT[:, :, :], rows(pb[1][:, 0:2 * P], P, 2)[:, :, 0:TAPS]).then_inc(s["wd_out"], 1)
                for t in range(TB):
                    bank = pb[4:8] if t == 0 else pb[0:4]
                    for n in range(2):
                        act.wait_ge(s["qkv_made"], 8 * l + 4 * t + n + 1)
                        copy(qrows[t][:, 4 * n:4 * n + 4, :], rows(bank[n][:, 0:4 * QK], P, 4)
                             ).then_inc(s["qkv_out"], 1)
                    for n in range(2):
                        act.wait_ge(s["qkv_made"], 8 * l + 4 * t + n + 3)
                        kv = rows(bank[2 + n], P, 4)
                        copy(krows[t][:, 4 * n:4 * n + 4, 0:NOPE], kv[:, :, 0:NOPE]).then_inc(s["qkv_out"], 1)
                        copy(vrows[t][:, 4 * n:4 * n + 4, :], kv[:, :, NOPE:NOPE + MV]).then_inc(s["qkv_out"], 1)
                if l == 0:
                    sums_out(2)
                for t in range(TB):
                    bank = pb[4:8] if t == 0 else pb[0:4]
                    for n in range(4):
                        act.wait_ge(s["hq_made"], 8 * l + 4 * t + n + 1)
                        to = (qTh, kTh)[n // 2]
                        copy(to[0:QK, 4 * (n % 2):4 * (n % 2) + 4, t * P:(t + 1) * P], rows(bank[n], QK, 4)
                             ).then_inc(s["hq_out"], 1)
                for t in range(TB):
                    lo = P if t == 0 else 0
                    if l == 0 and t == 1:
                        sums_out(3)
                        pool_sums_out(0, pb[1])
                    act.wait_ge(s["max_ready"], TB * l + t + 1)
                    f(sinkd[:, :], sinkd[:, :], ACT.Exp)
                    for a in range(AH):
                        e = f(S[:, a, lo:2 * P], S[:, a, lo:2 * P], ACT.Exp, bias=nmax[:, a:a + 1],
                              scale=MLA_SCALE if a < MH else SWA_SCALE, accum_out=rsum[:, a:a + 1])
                    e.then_inc(s["exp_out"], 1)
                    for n in range(3 if t == 0 else 6):
                        act.wait_ge(s["pT_made"], 9 * l + 3 * t + n + 1)
                        if t == 0:
                            copy(pT[:, 4 * n:4 * n + 4, 1, :], rows(pb[n], P, 4)).then_inc(s["pT_out"], 1)
                        else:
                            src = pb[3 + n] if n < 5 else pb[2]
                            copy(pT[:, 2 * n:2 * n + 2, :, :].rearrange("p a b c -> p (a b c)"), src[:, :]
                                 ).then_inc(s["pT_out"], 1)
                for b in range(4):
                    act.wait_ge(s["oT_made"], 4 * l + b + 1)
                    t, n = b // 2, b % 2
                    cut = slice(t * P, (t + 1) * P)
                    if n == 0:
                        e = copy(oT[:, 0:4, cut], rows(pb[3 + b], P, 4))
                    else:
                        e = copy(oT[:, 6:8, cut], rows(pb[3 + b][:, 0:2 * P], P, 2))
                    e.then_inc(s["oT_out"], 1)
                act.wait_ge(s["conv_col_made"], l + 1)
                for n in range(CC):
                    e = f(hnT[:, n, :], pb[2][:, n * SEQ:(n + 1) * SEQ], ACT.Silu,
                          bias=cols[:, 7 + n:8 + n], scale=cols[:, 5 + n:6 + n])
                e.then_inc(s["conv_act"], 1)
                act.wait_ge(s["conv_pw_made"], l + 1)
                for n in range(CC):
                    e = f(oT[:, 4 + n, :], pb[7][:, n * SEQ:(n + 1) * SEQ], ACT.Identity, bias=cols[:, 9 + n:10 + n])
                e.then_inc(s["conv_pw_out"], 1)
                rows_out(l, GT1_ROW, pb[5:7])
                rows_out(l, SC2_ROW, (pb[4], pb[7]))
                rows_out(l, SH2_ROW, pb[5:7])
                if l == 0:
                    pool_sums_out(1, pb[1])
                for b in range(4):
                    act.wait_ge(s["sk_made"], 4 * l + b + 1)
                    copy(skT[:, 4 * b:4 * b + 4, :], rows(pb[4 + b], P, 4)).then_inc(s["sk_out"], 1)

                def query_out(g):
                    hold(act, s["q_made"], g + (GROUPS * l + 1))
                    copy(qrow[:, :], Q_BANK[:, 0:2 * PK]).then_inc(s["q_out"], 1)
                    hold(act, s["qT_made"], g + (GROUPS * l + 1))
                    copy(qT2[:, :, :], rows(QS_BANK[:, 0:2 * P], P, 2)).then_inc(s["qT_out"], 1)

                def scores_out(g, t):
                    hold(act, s["s_made"], g + (GROUPS * l + 1))
                    copy(sc[:, t, :, :], rows(QS_BANK[:, 2 * P:4 * P], P, 2)).then_inc(s["s_out"], 1)

                def gate_exp(g, t):
                    hold(act, s["picks_ready"], g + (GROUPS * l + 1))
                    f(gexp[:, t, :], best[:, t, :], ACT.Exp, bias=nbest[:, t:t + 1],
                      accum_out=gsum[:, t:t + 1]).then_inc(s["gate_out"], 1)
                    f(warm[:, t:t + 1], cst[:, C_HALF:C_HALF + 1], ACT.Gelu)

                def gelu(g, t):
                    hold(act, s["u_used"], g * TOPK + (U_TURN * l + UR + TOPK))
                    f(gel[:, t, :], dots[:, t, :], ACT.Gelu).then_inc(s["gelu_out"], 1)

                def diagonals(i, t, ks):
                    for k in ks:
                        hold(act, s["v_used"], i * TOPK + (V_TURN * l + k + 1))
                        f(diag[:, k % VR, :], ident, ACT.Copy, scale=coef[:, t, k:k + 1]
                          ).then_inc(s["diag_ready"], 1)

                def body(it, i, j, last):
                    t = j % TB
                    hold(act, s["coef_ready"], i + (GROUPS * l + 1))
                    asks = not (last and j + 3 >= SPAN)
                    diagonals(i, t, range(12))
                    if asks:
                        query_out(i + 3)
                    diagonals(i, t, (12,))
                    if asks:
                        hold(act, s["idx_ready"], i + (GROUPS * l + 2))
                        scores_out(i + 3, (j + 3) % TB)
                    diagonals(i, t, (13,))
                    if not (last and j + 2 >= SPAN):
                        gate_exp(i + 2, t)
                    diagonals(i, t, (14, 15))
                    if last and l == 0:
                        for n in in_span(j):
                            late_out(n)
                    if not (last and j + 1 >= SPAN):
                        gelu(i + 1, (j + 1) % TB)

                for g in range(3):
                    t = g % TB
                    if g < TB:
                        for half in range(2):
                            act.wait_ge(s["h2T_made"], 4 * l + 2 * t + half + 1)
                            for k in range(4):
                                kk = 4 * half + k
                                e = f(hT[:, kk, t * P:(t + 1) * P], pb[2 * t + half][:, k * P:(k + 1) * P],
                                      ACT.Identity, scale=mcol(l, SC2, kk), bias=mcol(l, SH2, kk))
                            e.then_inc(s["h2T_out"], 1)
                    query_out(g)
                    if g == 2:
                        act.wait_ge(s["idx_ready"], GROUPS * l + 1)
                    scores_out(g, t)
                rows_out(l, GT2_ROW, ADA_BANK)
                gate_exp(0, 0)
                gate_exp(1, 1)
                gelu(0, 0)
                if l == 0:
                    for i in range(POOL_CHUNKS, IN_SPAN):
                        late_out(i)
                retrieval_loop(act, body)

        @block.vector
        def _(dve):
            v = nc.vector
            chain = Chain(dve, s["dve_chain"])
            roots = [0]

            def layer_norm(t, src_bank, gate, done):
                xt, ht = xs[:, t, :], h[:, t, :]
                for n in range(2):
                    cut = slice(n * 512, (n + 1) * 512)
                    chain(v.scalar_tensor_tensor(ht[:, cut], gate[:, cut], 1.0, src_bank[n][:, :],
                                                 ALU.add, ALU.mult))
                chain.sync()
                chain(v.scalar_tensor_tensor(xt, xt, ALPHA, ht, ALU.mult, ALU.add))
                chain.sync()
                norm_stats(xt, D)
                e = v.tensor_scalar(xt, xt, stat[:, 12:13], stat[:, 13:14], ALU.subtract, ALU.mult)
                if done is None:
                    chain(e)
                    chain.sync()
                else:
                    e.then_inc(done, 1)

            def gain_and_offset(to, t, gain, offset, done):
                chain(v.tensor_tensor(to[:, t, :], xs[:, t, :], gain, ALU.mult))
                chain.sync()
                v.tensor_tensor(to[:, t, :], to[:, t, :], offset, ALU.add).then_inc(done, 1)

            def add_offsets(l, lo, hi):
                chain(v.tensor_tensor(modc[:, l, lo:hi], modc[:, l, lo:hi],
                                      colT[:, l * COLS_B + lo:l * COLS_B + hi], ALU.add))
                chain.sync()

            def ln_cols(which, l):
                lo = LAYERS * COLS_B + (which * LAYERS + l) * KC
                return colT[:, lo:lo + KC]

            def fold(l, scale, shift, gain, offset):
                scale = modc[:, l, scale * KC:(scale + 1) * KC]
                shift = modc[:, l, shift * KC:(shift + 1) * KC]
                chain(v.scalar_tensor_tensor(lift[:, :], scale, 1.0, offset, ALU.add, ALU.mult))
                chain.sync()
                chain(v.tensor_tensor(shift, shift, lift[:, :], ALU.add))
                chain(v.scalar_tensor_tensor(scale, scale, 1.0, gain, ALU.add, ALU.mult))
                chain.sync()

            def norm_stats(src, n):
                parts = max(1, n // 512)
                for q in range(parts):
                    chain(v.bn_stats(stat[:, 6 * q:6 * q + 6], src[:, q * (n // parts):(q + 1) * (n // parts)]))
                chain.sync()
                chain(v.bn_aggr(stat[:, 12:14], stat[:, 0:6 * parts]))
                chain.sync()
                v.tensor_scalar(stat[:, 13:14], stat[:, 13:14], EPS, None, ALU.add).then_inc(s["var_ready"], 1)
                roots[0] += 1
                dve.wait_ge(s["root_out"], roots[0])

            def terms(i):
                if i < ADA_FIRST:
                    dve.wait_ge(first_in[i], 16)
                else:
                    dve.wait_ge(s[f"ada_in{i % 2}"], 16 * ((i - ADA_FIRST) // 2 + 1))
                if i >= 4:
                    dve.wait_ge(s["ada_made"], i - 3)
                w, place = ada_tile(i), terms_place(i)
                for k in range(KC):
                    if k == 0:
                        e = v.tensor_scalar(place, w[:, k, :], ccol[:, k:k + 1], None, ALU.mult)
                    else:
                        chain.sync()
                        e = v.scalar_tensor_tensor(place, w[:, k, :], ccol[:, k:k + 1], place, ALU.mult, ALU.add)
                    if k < KC - 1:
                        chain(e)
                    else:
                        e.then_inc(s["terms_ready"], 1)

            dve.wait_ge(s["consts_in"], 16)
            dve.wait_ge(s["cs_ready"], 1)
            for i in range(ADA_FIRST):
                terms(i)
            dve.wait_ge(s["cols_out"], 1)

            for l in range(LAYERS):
                if l == 0:
                    dve.wait_ge(s["ada_out"], ADA_FIRST)
                    add_offsets(0, 0, ADA_FIRST * ADA_C)
                    first = modc[:, 0, SC1 * KC:(SC1 + 1) * KC]
                    v.tensor_scalar(first, first, 1.0, None, ALU.add).then_inc(s["cols_ready"], 1)
                    dve.wait_ge(s["cols_ready"], 1)
                for t in range(TB):
                    dve.wait_ge(s["hT_made"], 4 * l + 2 * t + 2)
                    for k in range(4, KC):
                        e = v.tensor_scalar(hT[:, k, t * P:(t + 1) * P], pb[2 * t + 1][:, (k - 4) * P:(k - 3) * P],
                                            mcol(l, SC1, k), mcol(l, SH1, k), ALU.mult, ALU.add)
                    e.then_inc(s["hTd_out"], 1)
                if l == 0:
                    terms(6)
                for t in range(TB):
                    if l == 0 and t == 1:
                        for i in range(7, 12):
                            terms(i)
                    dve.wait_ge(s["proj_out"], 6 * l + 3 * t + 1)
                    if t == 0:
                        chain.sync()
                    parts = ((O_CQ, Q_RANK, 0), (O_CKV, KV_RANK, 1))
                    for lo, n, q in parts:
                        p_ = proj[:, t, lo:lo + n]
                        chain(v.scalar_tensor_tensor(junk[:, lo:lo + n], p_, 1.0, p_, ALU.mult, ALU.mult,
                                                     accum_out=stat[:, q:q + 1]))
                    chain.sync()
                    for lo, n, q in parts:
                        e = v.tensor_scalar(stat[:, q:q + 1], stat[:, q:q + 1], 1.0 / n, EPS, ALU.mult, ALU.add)
                        if q == 0:
                            chain(e)
                        else:
                            e.then_inc(s["var_ready"], 1)
                    roots[0] += 1
                    dve.wait_ge(s["root_out"], roots[0])
                    for lo, n, q in parts:
                        p_ = proj[:, t, lo:lo + n]
                        e = v.tensor_scalar(p_, p_, stat[:, q:q + 1], None, ALU.mult)
                        if q == 0:
                            chain(e)
                        else:
                            e.then_inc(s["rms_ready"], 1)
                    dve.wait_ge(s["rms_ready"], TB * l + t + 1)
                dve.wait_ge(s["glu_sig"], l + 1)
                a_ = proj[:, :, O_CONV:O_CONV + CONV]
                v.tensor_tensor(a_, a_, proj[:, :, O_CONV + CONV:O_CONV + 2 * CONV], ALU.mult
                                ).then_inc(s["glu_ready"], 1)
                chain(v.memset(hc[:, :, 0:PAD], 0.0))
                if l == 0:
                    terms(12)
                half = ROPE // 2
                for t in range(TB):
                    cos = cst[:, C_COS + t * half:C_COS + (t + 1) * half]
                    sin = cst[:, C_SIN + t * half:C_SIN + (t + 1) * half]
                    k1 = proj[:, t, O_KR:O_KR + half]
                    k2 = proj[:, t, O_KR + half:O_KR + ROPE]
                    for q, (a_, b_) in enumerate(((k1, cos), (k2, sin), (k1, sin), (k2, cos))):
                        chain(v.tensor_tensor(krot[:, q, :], a_, b_, ALU.mult))
                    chain.sync()
                    chain(v.tensor_tensor(krot[:, 0, :], krot[:, 0, :], krot[:, 1, :], ALU.subtract))
                    chain(v.tensor_tensor(krot[:, 2, :], krot[:, 2, :], krot[:, 3, :], ALU.add))
                    chain.sync()
                    chain(v.tensor_copy(krows[t][:, :, NOPE:NOPE + half], over(krot[:, 0, :], MH)))
                    chain(v.tensor_copy(krows[t][:, :, NOPE + half:QK], over(krot[:, 2, :], MH)))
                    chain.sync()
                    dve.wait_ge(s["qkv_out"], 12 * l + 6 * t + 2)
                    q1 = qrows[t][:, :, NOPE:NOPE + half]
                    q2 = qrows[t][:, :, NOPE + half:QK]
                    tmp = [rows(junk[:, q * MH * half:(q + 1) * MH * half], P, MH) for q in range(4)]
                    for q, (a_, b_) in enumerate(((q1, cos), (q2, sin), (q1, sin), (q2, cos))):
                        chain(v.tensor_tensor(tmp[q], a_, over(b_, MH), ALU.mult))
                    chain.sync()
                    chain(v.tensor_tensor(q1, tmp[0], tmp[1], ALU.subtract))
                    v.tensor_tensor(q2, tmp[2], tmp[3], ALU.add).then_inc(s["rope_ready"], 1)
                    dve.wait_ge(s["rope_ready"], TB * l + t + 1)

                def taps(k0, k1):
                    for k in range(k0, k1):
                        for n in range(CC):
                            src = hc[:, n, k:k + SEQ]
                            if k == 0:
                                chain(v.tensor_scalar(cacc[:, n, :], src, wdT[:, n, 0:1], cols[:, 3 + n:4 + n],
                                                      ALU.mult, ALU.add))
                            else:
                                chain(v.scalar_tensor_tensor(cacc[:, n, :], src, wdT[:, n, k:k + 1],
                                                             cacc[:, n, :], ALU.mult, ALU.add))
                        chain.sync()

                dve.wait_ge(s["conv_in_out"], l + 1)
                dve.wait_ge(s["wd_out"], l + 1)
                dve.wait_ge(s["small_in"], 16 * SMALL_LOADS * (l + 1))
                if l == 0:
                    for i in (13, 14, 15):
                        terms(i)
                taps(0, 2)

                for t in range(TB):
                    if t:
                        dve.wait_ge(s["pT_made"], 9 * l + 3)
                    for n in range(3 if t == 0 else 6):
                        dve.wait_ge(s["sc_made"], 9 * l + 3 * t + n + 1)
                        if t == 0:
                            e = v.tensor_tensor(S[:, 4 * n:4 * n + 4, P:2 * P], rows(pb[n], P, 4),
                                                over(own_mask, 4), ALU.add)
                        else:
                            src = pb[3 + n] if n < 5 else pb[2]
                            e = v.tensor_tensor(S[:, 2 * n:2 * n + 2, :], rows(src, P, 2),
                                                over(full_mask if n < 4 else band_mask, 2), ALU.add)
                        e.then_inc(s["mask_out"], 1)
                    dve.wait_ge(s["mask_out"], 9 * l + (3 if t == 0 else 9))
                    chain(v.tensor_reduce(rowmax[:, :], S[:, :, P if t == 0 else 0:2 * P], AX.X, ALU.max))
                    chain.sync()
                    chain(v.tensor_scalar(nmax[:, 0:MH], rowmax[:, 0:MH], -MLA_SCALE, None, ALU.mult))
                    chain(v.scalar_tensor_tensor(rowmax[:, MH:AH], rowmax[:, MH:AH], SWA_SCALE, sinkb[:, :],
                                                 ALU.mult, ALU.max))
                    chain.sync()
                    chain(v.tensor_scalar(nmax[:, MH:AH], rowmax[:, MH:AH], -1.0, None, ALU.mult))
                    v.tensor_tensor(sinkd[:, :], sinkb[:, :], rowmax[:, MH:AH], ALU.subtract
                                    ).then_inc(s["max_ready"], 1)
                    taps(2 if t == 0 else 14, 14 if t == 0 else TAPS)
                    dve.wait_ge(s["exp_out"], TB * l + t + 1)
                    chain(v.tensor_tensor(rsum[:, MH:AH], rsum[:, MH:AH], sinkd[:, :], ALU.add))
                    chain.sync()
                    chain(v.reciprocal(rinv[:, t, :], rsum[:, :]))
                    chain.sync()
                    dve.wait_ge(s["o_made"], TB * l + t + 1)
                    chain(v.tensor_tensor(rows(orow[:, t, 0:512], P, MH), rows(pb[0], P, MH),
                                          each(rinv[:, t, 0:MH], MV), ALU.mult))
                    v.tensor_tensor(rows(orow[:, t, 512:768], P, SH), rows(pb[1][:, 0:256], P, SH),
                                    each(rinv[:, t, MH:AH], SD), ALU.mult).then_inc(s["o_out"], 1)
                chain.sync()
                if l == 0:
                    dve.wait_ge(s["ada_out"], GROUPS)
                    add_offsets(0, ADA_FIRST * ADA_C, COLS_B)
                    fold(0, SC2, SH2, ln_cols(0, 0), ln_cols(1, 0))
                    dve.sem_inc(s["cols_ready"], 1)
                dve.wait_ge(s["conv_row_made"], l + 1)
                for t in range(TB):
                    norm_stats(pb[7][:, t * CONV:(t + 1) * CONV], CONV)
                    chain(v.tensor_scalar(crow[:, t, :], pb[7][:, t * CONV:(t + 1) * CONV], stat[:, 12:13],
                                          stat[:, 13:14], ALU.subtract, ALU.mult))
                    chain.sync()
                dve.sem_inc(s["conv_norm"], 1)
                dve.wait_ge(s["oT_made"], 4 * (l + 1))
                if l:
                    dve.wait_ge(s["ln2_done"], TB * l)
                for t in range(TB):
                    dve.wait_ge(s["mix_made"], TB * l + t + 1)
                    bank = pb[2 * t:2 * t + 2]
                    dve.wait_ge(s["rep_out"], 4 * l + GT1_ROW + 1)
                    layer_norm(t, bank, mods[:, GT1_ROW, :], s["hn_ready"])
                    dve.wait_ge(s["hn_ready"], TB * l + t + 1)
                    dve.wait_ge(s["rep_out"], 4 * l + SH2_ROW + 1)
                    gain_and_offset(h, t, mods[:, SC2_ROW, :], mods[:, SH2_ROW, :], s["h2_ready"])

                def picks(g, t, part):
                    chain.sync()
                    if part == 0:
                        hold(dve, s["s_out"], g + (GROUPS * l + 1))
                        for q in range(2):
                            chain(v.max(top[:, q, 0:8], sc[:, t, q, :]))
                        chain.sync()
                        for q in range(2):
                            chain(v.max_index(topi[:, q, 0:8], top[:, q, 0:8], sc[:, t, q, :]))
                    elif part == 1:
                        for q in range(2):
                            chain(v.match_replace(sc[:, t, q, :], top[:, q, 0:8], sc[:, t, q, :], LOWEST))
                        chain.sync()
                        for q in range(2):
                            chain(v.max(top[:, q, 8:16], sc[:, t, q, :]))
                    elif part == 2:
                        for q in range(2):
                            chain(v.max_index(topi[:, q, 8:16], top[:, q, 8:16], sc[:, t, q, :]))
                        pairs(cand, top)
                        chain.sync()
                        chain(v.tensor_copy(topf[:, :, :], topi[:, :, :]))
                        chain(v.max(best[:, t, 0:8], cand[:, :]))
                    elif part == 3:
                        chain(v.tensor_scalar(topf[:, 0, :], topf[:, 0, :], float(NSUB), float(NEXP * l),
                                              ALU.mult, ALU.add))
                        chain(v.max_index(pos[:, 0:8], best[:, t, 0:8], cand[:, :]))
                        chain.sync()
                        chain(v.match_replace(cand[:, :], best[:, t, 0:8], cand[:, :], LOWEST))
                        pairs(cide, topf)
                    elif part == 4:
                        chain(v.max(best[:, t, 8:16], cand[:, :]))
                        chain.sync()
                        chain(v.max_index(pos[:, 8:16], best[:, t, 8:16], cand[:, :]))
                        v.tensor_scalar(nbest[:, t:t + 1], best[:, t, 0:1], -1.0, None, ALU.mult
                                        ).then_inc(s["picks_ready"], 1)
                        chain.sync()
                        chain(v.tensor_copy(posf[:, :], pos[:, :]))
                    elif part < 7:
                        lo = (part - 5) * (TOPK // 2)
                        cut = slice(lo, lo + TOPK // 2)
                        chain(v.tensor_tensor(eq, each(posf[:, cut], NCAND), over(iota_row, TOPK // 2), ALU.is_equal))
                        chain.sync()
                        chain(v.tensor_tensor(eq, eq, over(cide[:, :], TOPK // 2), ALU.mult))
                        chain.sync()
                        chain(v.tensor_reduce(eidf[:, cut], eq, AX.X, ALU.add))
                    else:
                        v.tensor_copy(uidx[:, t, :], eidf[:, :]).then_inc(s["idx_ready"], 1)

                def pairs(to, of):
                    lo = 0
                    for a, na, nb in RECTS:
                        chain(v.tensor_tensor(rows(to[:, lo:lo + na * nb], P, na), each(of[:, 0, a:a + na], nb),
                                              over(of[:, 1, 0:nb], na), ALU.add))
                        lo += na * nb

                def product(g, t, k):
                    uses = TOPK // UR
                    hold(dve, u_in[k % UR], (g * uses) * 16 + 16 * (GROUPS * uses * l + k // UR + 1))
                    v.scalar_tensor_tensor(ring[:, k % UR, :], ring[:, k % UR, :], 1.0, h[:, t, :], ALU.mult,
                                           ALU.mult, accum_out=dots[:, t, k:k + 1]).then_inc(s["u_used"], 1)

                def coefficients(g, t):
                    hold(dve, s["gate_out"], g + (GROUPS * l + 1))
                    chain(v.reciprocal(ginv[:, t:t + 1], gsum[:, t:t + 1]))
                    hold(dve, s["gelu_out"], g + (GROUPS * l + 1))
                    chain.sync()
                    v.scalar_tensor_tensor(coef[:, t, :], gel[:, t, :], ginv[:, t:t + 1], gexp[:, t, :],
                                           ALU.mult, ALU.mult).then_inc(s["coef_ready"], 1)

                def body(it, i, j, last):
                    t = (j + 1) % TB
                    if not (last and j + 1 >= SPAN):
                        for k in range(TOPK):
                            product(i + 1, t, k)
                            if k == 4:
                                hold(dve, s["v_used"], i * TOPK + (V_TURN * l + VR))
                                hold(dve, s["idx_ready"], i + (GROUPS * l + 2))
                                v.tensor_copy(vidx[:, t, :], uidx[:, t, :]).then_inc(s["vidx_ready"], 1)
                            if k < PICK_PARTS and not (last and j + 2 >= SPAN):
                                picks(i + 2, j % TB, k)
                        coefficients(i + 1, t)

                dve.wait_ge(s["h2_ready"], TB * (l + 1))
                for part in range(PICK_PARTS):
                    picks(0, 0, part)
                dve.sem_inc(s["u_used"], UR)
                dve.wait_ge(s["idx_ready"], GROUPS * l + 1)
                v.tensor_copy(vidx[:, 0, :], uidx[:, 0, :]).then_inc(s["vidx_ready"], 1)
                for k in range(TOPK):
                    product(0, 0, k)
                    if k < PICK_PARTS:
                        picks(1, 1, k)
                coefficients(0, 0)
                retrieval_loop(dve, body, chain, DVE_STEPS)
                dve.wait_ge(s["ln1_done"], TB * (l + 1))
                dve.wait_ge(s["rep_out"], 4 * l + GT2_ROW + 1)
                if l + 1 < LAYERS:
                    dve.wait_ge(s["pool_out"], 2)
                    dve.wait_ge(s["late_out"], GROUPS - POOL_CHUNKS)
                    add_offsets(l + 1, 0, COLS_B)
                    fold(l + 1, SC1, SH1, ln_cols(2, l), ln_cols(3, l))
                    fold(l + 1, SC2, SH2, ln_cols(0, l + 1), ln_cols(1, l + 1))
                    dve.sem_inc(s["cols_ready"], 1)
                else:
                    dve.wait_ge(s["ln_in"], 64 * (l + 1))
                for t in range(TB):
                    dve.wait_ge(s["y_made"], TB * l + t + 1)
                    if l + 1 < LAYERS:
                        layer_norm(t, Y[t], mods[:, GT2_ROW, :], s["xn_ready"])
                        dve.wait_ge(s["xn_ready"], TB * l + t + 1)
                    else:
                        layer_norm(t, Y[t], mods[:, GT2_ROW, :], None)
                        gain_and_offset(xs, t, lnr[:, 0, :], lnr[:, 1, :], s["ln2_done"])

        @block.tensor
        def _(pe):
            mm = nc.tensor.matmul
            tr = nc.tensor.transpose

            def late(i):
                pe.wait_ge(s[f"late_in{i % 2}"], 16 * ((i - POOL_CHUNKS) // 2 + 1))
                if i > POOL_CHUNKS + 1:
                    pe.wait_ge(s["late_out"], i - POOL_CHUNKS - 1)
                for m in range(ADA_C):
                    for k in range(KC):
                        e = mm(ADA_BANK[i % 2][:, m:m + 1], ada_w[i % 2][:, k, m * P:(m + 1) * P], ccol[:, k:k + 1],
                               start=k == 0, stop=k == KC - 1)
                e.then_inc(s["late_made"], 1)

            def pool_sums(chunks, bank):
                pe.wait_ge(s["pool_terms"], chunks[-1] + 1)
                for q in chunks:
                    for m in range(ADA_C):
                        col = (q - chunks[0]) * ADA_C + m
                        e = mm(bank[:, col:col + 1], pool_place(q)[:, m * P:(m + 1) * P], ones_col, start=True, stop=True)
                e.then_inc(s["pool_made"], 1)

            def sums(chunks):
                for i in chunks:
                    batch, bank = next(b for b in sum_batches if i in b[0])
                    pe.wait_ge(s["terms_ready"], i + 1)
                    for m in range(ADA_C):
                        col = (i - batch[0]) * ADA_C + m
                        e = mm(bank[:, col:col + 1], terms_place(i)[:, m * P:(m + 1) * P], ones_col, start=True, stop=True)
                    e.then_inc(s["ada_made"], 1)

            def spread(l, part, of, banks):
                for k in range(KC):
                    e = mm(banks[k // 4][:, (k % 4) * P:(k % 4 + 1) * P], mcol(l, of, k).to_broadcast([P, P]), ident,
                           start=True, stop=True)
                e.then_inc(s["rep_made"], 1)

            pe.wait_ge(s["consts_in"], 16)
            pe.wait_ge(s["rows_in"], 16 * 5)
            tr(pb[0][:, 0:LAYERS * COLS_B], raw_b, ident[0:LAYERS * COLS_B, 0:LAYERS * COLS_B])
            n = 4 * LAYERS * KC
            tr(pb[1][:, 0:n], raw_ln, ident[0:n, 0:n]).then_inc(s["cols_made"], 1)
            sums(range(ADA_FIRST))
            pe.wait_ge(s["cols_out"], 1)

            for l in range(LAYERS):
                for b in range(4):
                    t, half = b // 2, b % 2
                    if l == 0:
                        pe.wait_ge(s["x_in"], 16)
                    else:
                        pe.wait_ge(s["xn_ready"], TB * (l - 1) + t + 1)
                    for k in range(4):
                        kk = 4 * half + k
                        e = tr(pb[b][:, k * P:(k + 1) * P], xs[:, t, kk * P:(kk + 1) * P], ident)
                    e.then_inc(s["hT_made"], 1)
                pe.wait_ge(s["win_in"], 16 * (l + 1))
                if l == 0:
                    pe.wait_ge(s["ada_out"], ADA_FIRST)
                for b in range(6):
                    t, n = b // 3, b % 3
                    pe.wait_ge(s["hT_out"], TB * l + (t + 1 if b < 4 else TB))
                    pe.wait_ge(s["hTd_out"], TB * l + (t + 1 if b < 4 else TB))
                    to = pb[(4 + b) % 8 if b < 4 else b - 4][:, 0:PROJ_N]
                    for k in range(KC):
                        e = mm(to, hT[:, k, t * P:(t + 1) * P], win_w[:, k, n * PROJ_N:(n + 1) * PROJ_N],
                               start=k == 0, stop=k == KC - 1)
                    e.then_inc(s["proj_made"], 1)
                    if l == 0:
                        if b == 1:
                            pe.wait_ge(s["hT_out"], TB)
                        sums(sums_behind_projection.get(b, ()))
                for t in range(TB):
                    pe.wait_ge(s["proj_out"], 6 * l + (3 if t == 0 else 6))
                    if t == 0:
                        pe.wait_ge(s["proj_out"], 6 * l + 3)
                    for a in range(SH):
                        e = tr(pb[4 + 2 * t][0:SD, a * P:(a + 1) * P], proj[:, t, O_QS + a * SD:O_QS + (a + 1) * SD], ident)
                    e.then_inc(s["sw_made"], 1)
                    for a in range(SKV):
                        e = tr(pb[5 + 2 * t][0:SD, a * P:(a + 1) * P], proj[:, t, O_KS + a * SD:O_KS + (a + 1) * SD], ident)
                    e.then_inc(s["sw_made"], 1)
                for t in range(TB):
                    pe.wait_ge(s["rms_ready"], TB * l + t + 1)
                    if l == 0 and t == 0:
                        pe.wait_ge(s["ada_out"], 1 + sum_batches[1][0][-1])
                    for n in range(3):
                        e = tr(pb[2 + t][:, n * P:(n + 1) * P], proj[:, t, n * P:(n + 1) * P], ident)
                    e.then_inc(s["cn_made"], 1)
                pe.wait_ge(s["glu_ready"], l + 1)
                for n in range(CC):
                    for t in range(TB):
                        e = tr(pb[0][:, (TB * n + t) * P:(TB * n + t + 1) * P],
                               proj[:, t, O_CONV + n * P:O_CONV + (n + 1) * P], ident)
                e.then_inc(s["conv_in_made"], 1)
                pe.wait_ge(s["wdr_in"], 16 * (l + 1))
                for n in range(CC):
                    e = tr(pb[1][:, n * P:n * P + TAPS], wdraw[0:TAPS, n * P:(n + 1) * P], ident[0:TAPS, 0:TAPS])
                e.then_inc(s["wd_made"], 1)
                pe.wait_ge(s["small_in"], 16 * SMALL_LOADS * (l + 1))
                pe.wait_ge(s["sw_out"], 4 * (l + 1))
                for t in range(TB):
                    bank = pb[4:8] if t == 0 else pb[0:4]
                    cut = slice(t * P, (t + 1) * P)
                    pe.wait_ge(s["cn_out"], TB * l + (1 if t == 0 else TB))
                    if t:
                        pe.wait_ge(s["wd_out"], l + 1)
                    for n in range(2):
                        for k in range(2):
                            e = mm(bank[n][:, 0:4 * QK], cqT[:, k, cut], wuq[:, k, n * 4 * QK:(n + 1) * 4 * QK],
                                   start=k == 0, stop=k == 1)
                        e.then_inc(s["qkv_made"], 1)
                    for n in range(2):
                        mm(bank[2 + n][:, :], ckvT[:, cut], wukv[:, n * 512:(n + 1) * 512], start=True, stop=True
                           ).then_inc(s["qkv_made"], 1)
                if l == 0:
                    pe.wait_ge(s["qkv_out"], 6)
                    sums(sums_behind_qkv)
                for t in range(TB):
                    bank = pb[4:8] if t == 0 else pb[0:4]
                    pe.wait_ge(s["qkv_out"], 12 * l + 6 * (t + 1))
                    pe.wait_ge(s["rope_ready"], TB * l + t + 1)
                    for n in range(4):
                        if l == 0 and t == 0 and n == 3:
                            pe.wait_ge(s["ada_out"], 1 + sums_behind_qkv[-1])
                        src = (qrows, krows)[n // 2][t]
                        for a in range(4):
                            e = tr(bank[n][0:QK, a * P:(a + 1) * P], src[:, 4 * (n % 2) + a, :], ident)
                        e.then_inc(s["hq_made"], 1)

                def scores(t, a, to):
                    n = P if t == 0 else 2 * P
                    q_, k_, w = (qTh[0:QK, a], kTh[0:QK, a], QK) if a < MH else \
                        (qsT[0:SD, a - MH], ksT[0:SD, (a - MH) // 2], SD)
                    return mm(to, q_[:, t * P:(t + 1) * P], k_[:, 0:n], start=True, stop=True)

                pe.wait_ge(s["hq_out"], 8 * (l + 1))
                for n in range(3):
                    for a in range(4):
                        e = scores(0, 4 * n + a, pb[n][:, a * P:(a + 1) * P])
                    e.then_inc(s["sc_made"], 1)
                for n in range(4):
                    for a in range(2):
                        e = scores(1, 2 * n + a, pb[3 + n][:, a * 2 * P:(a + 1) * 2 * P])
                    e.then_inc(s["sc_made"], 1)
                pe.wait_ge(s["exp_out"], TB * l + 1)
                pe.wait_ge(s["mask_out"], 9 * l + 3)
                for n in range(3):
                    for a in range(4):
                        e = tr(pb[n][:, a * P:(a + 1) * P], S[:, 4 * n + a, P:2 * P], ident)
                    e.then_inc(s["pT_made"], 1)

                def outputs(t):
                    for a in range(AH):
                        to = pb[0][:, a * MV:(a + 1) * MV] if a < MH else pb[1][:, (a - MH) * SD:(a - MH + 1) * SD]
                        for kb in range(0 if t else 1, 2):
                            blk = t if kb else 0
                            val = vrows[blk][:, a, :] if a < MH else \
                                proj[:, blk, O_VS + (a - MH) // 2 * SD:O_VS + ((a - MH) // 2 + 1) * SD]
                            e = mm(to, pT[:, a, kb, :], val, start=kb == 0 or t == 0, stop=kb == 1)
                    e.then_inc(s["o_made"], 1)

                pe.wait_ge(s["pT_out"], 9 * l + 3)
                outputs(0)
                for n in range(4, 6):
                    to = pb[7] if n == 4 else pb[2]
                    for a in range(2):
                        e = scores(1, 2 * n + a, to[:, a * 2 * P:(a + 1) * 2 * P])
                    e.then_inc(s["sc_made"], 1)
                if l == 0:
                    pe.wait_ge(s["o_out"], 1)
                    sums(sums_behind_scores)
                    pool_sums(range(POOL_BATCH), pb[1])
                    pe.wait_ge(s["pool_out"], 1)
                pe.wait_ge(s["exp_out"], TB * (l + 1))
                for n in range(6):
                    to = pb[3 + n] if n < 5 else pb[2]
                    for a in range(2):
                        for kb in range(2):
                            e = tr(to[:, (2 * a + kb) * P:(2 * a + kb + 1) * P], S[:, 2 * n + a, kb * P:(kb + 1) * P], ident)
                    e.then_inc(s["pT_made"], 1)
                pe.wait_ge(s["pT_out"], 9 * (l + 1))
                pe.wait_ge(s["o_out"], TB * l + 1)
                outputs(1)
                pe.wait_ge(s["o_out"], TB * (l + 1))
                for t in range(TB):
                    for n in range(CC):
                        e = tr(pb[7][:, t * CONV + n * P:t * CONV + (n + 1) * P], cacc[:, n, t * P:(t + 1) * P], ident)
                e.then_inc(s["conv_row_made"], 1)
                for t in range(TB):
                    for n in range(6):
                        to = pb[3 + 2 * t] if n < 4 else pb[4 + 2 * t]
                        e = tr(to[:, (n % 4) * P:(n % 4 + 1) * P], orow[:, t, n * P:(n + 1) * P], ident)
                        if n in (3, 5):
                            e.then_inc(s["oT_made"], 1)
                def output_product(t, n, ks, first=False, last=False):
                    for k in ks:
                        e = mm(pb[2 * t + n][:, :], oT[:, k, t * P:(t + 1) * P], wo_w[:, k, n * 512:(n + 1) * 512],
                               start=first and k == ks[0], stop=last and k == ks[-1])
                    return e

                of_attention, of_conv = (0, 1, 2, 3, 6, 7), (4, 5)
                pe.wait_ge(s["wo_in"], 16 * (l + 1))
                pe.wait_ge(s["oT_out"], 4 * l + 2)
                output_product(0, 0, of_attention, first=True)
                pe.wait_ge(s["conv_norm"], l + 1)
                for n in range(CC):
                    for t in range(TB):
                        e = tr(pb[2][:, (TB * n + t) * P:(TB * n + t + 1) * P], crow[:, t, n * P:(n + 1) * P], ident)
                e.then_inc(s["conv_col_made"], 1)
                output_product(0, 1, of_attention, first=True)
                pe.wait_ge(s["conv_act"], l + 1)
                for n in range(CC):
                    for k in range(CC):
                        e = mm(pb[7][:, n * SEQ:(n + 1) * SEQ], wpw[:, k, n * P:(n + 1) * P], hnT[:, k, :],
                               start=k == 0, stop=k == CC - 1)
                e.then_inc(s["conv_pw_made"], 1)
                pe.wait_ge(s["oT_out"], 4 * (l + 1))
                pe.wait_ge(s["cols_ready"], l + 2)
                spread(l, GT1_ROW, GT1, pb[5:7])
                pe.wait_ge(s["conv_pw_out"], l + 1)
                for n in range(2):
                    e = output_product(0, n, of_conv, last=True)
                e.then_inc(s["mix_made"], 1)
                output_product(1, 0, range(KC), first=True, last=True)
                spread(l, SC2_ROW, SC2, (pb[4], pb[7]))
                pe.wait_ge(s["rep_out"], 4 * l + GT1_ROW + 1)
                spread(l, SH2_ROW, SH2, pb[5:7])
                output_product(1, 1, range(KC), first=True, last=True).then_inc(s["mix_made"], 1)
                if l == 0:
                    pe.wait_ge(s["hn_ready"], 1)
                    pool_sums(range(POOL_BATCH, POOL_CHUNKS), pb[1])
                pe.wait_ge(s["skr_in"], 16 * (l + 1))
                pe.wait_ge(s["rep_out"], 4 * l + SH2_ROW + 1)
                for b in range(4):
                    for k in range(4):
                        e = tr(pb[4 + b][:, k * P:(k + 1) * P], sk_raw[:, 4 * b + k, :], ident)
                    e.then_inc(s["sk_made"], 1)
                pe.wait_ge(s["sk_out"], 4 * (l + 1))

                def query_products(g, t, slot, turn, ks):
                    if ks[0] == 0:
                        hold(pe, s[f"wpq_in{slot}"], turn)
                        if not (isinstance(g, int) and g == 0):
                            hold(pe, s["s_out"], g + GROUPS * l)
                    for k in ks:
                        e = mm(Q_BANK[:, 0:2 * PK], hT[:, k, t * P:(t + 1) * P], wpq_w[slot][:, k, :],
                               start=k == 0, stop=k == KC - 1)
                    if ks[-1] == KC - 1:
                        e.then_inc(s["q_made"], 1)

                def query_transposes(g):
                    hold(pe, s["q_out"], g + (GROUPS * l + 1))
                    for q in range(2):
                        e = tr(QS_BANK[:, q * P:(q + 1) * P], qrow[:, q * PK:(q + 1) * PK], ident)
                    e.then_inc(s["qT_made"], 1)

                def query_scores(g, head):
                    hold(pe, s["qT_out"], g + (GROUPS * l + 1))
                    for q in range(2):
                        keys = skT[:, bass.ds(head * 2 + q, 1), :].rearrange("p a n -> p (a n)")
                        e = mm(QS_BANK[:, (2 + q) * P:(3 + q) * P], qT2[:, q, :], keys, start=True, stop=True)
                    e.then_inc(s["s_made"], 1)

                def weigh(i, t, k):
                    uses = TOPK // VR
                    hold(pe, v_in[k % VR], (i * uses) * 16 + 16 * (GROUPS * uses * l + k // VR + 1))
                    hold(pe, s["diag_ready"], i * TOPK + (PICKS * l + k + 1))
                    for n in range(2):
                        e = mm(Y[t][n][:, :], diag[:, k % VR, :], ring[:, UR + k % VR, n * 512:(n + 1) * 512],
                               start=False, stop=False)
                    e.then_inc(s["v_used"], 1)

                def body(it, i, j, last):
                    t = j % TB
                    asks = not (last and j + 3 >= SPAN)
                    hd = (j + 3) // TB
                    for k in range(TOPK):
                        if asks and 4 <= k < 8:
                            query_products(i + 3, (j + 3) % TB, hd % 2,
                                           it * 16 + 16 * (PH // 2 * l + (j + 3) // SPAN + 1),
                                           range(2 * k - 8, 2 * k - 6))
                        weigh(i, t, k)
                        if asks and k == 8:
                            query_transposes(i + 3)
                        if asks and k == 9:
                            query_scores(i + 3, it * (SPAN // TB) + hd)
                        if last and l == 0 and k in (7, 10, 13)[:len(in_span(j))]:
                            late(in_span(j)[(k - 7) // 3])
                    if last and j >= SPAN - TB:
                        for n in range(2):
                            e = mm(Y[t][n][:, :], zero_row, any_row, start=False, stop=True)
                        e.then_inc(s["y_made"], 1)

                for g in range(3):
                    t = g % TB
                    if g < TB:
                        pe.wait_ge(s["hn_ready"], TB * l + t + 1)
                        for half in range(2):
                            for k in range(4):
                                kk = 4 * half + k
                                e = tr(pb[2 * t + half][:, k * P:(k + 1) * P], xs[:, t, kk * P:(kk + 1) * P], ident)
                            e.then_inc(s["h2T_made"], 1)
                        pe.wait_ge(s["h2T_out"], 4 * l + 2 * (t + 1))
                    query_products(g, t, (g // TB) % 2, 16 * (PH // 2 * l + 1), range(KC))
                    query_transposes(g)
                    query_scores(g, g // TB)
                for t in range(TB):
                    for n in range(2):
                        e = mm(Y[t][n][:, :], zero_row, any_row, start=True, stop=False)
                spread(l, GT2_ROW, GT2, ADA_BANK)
                pe.wait_ge(s["rep_out"], 4 * l + GT2_ROW + 1)
                if l == 0:
                    for i in range(POOL_CHUNKS, IN_SPAN):
                        late(i)
                pe.sem_inc(s["v_used"], VR)
                retrieval_loop(pe, body)


def shape_constants(np):
    k = np.zeros((P, C_END), np.float32)
    i, j = np.arange(P)[:, None], np.arange(P)[None, :]
    k[:, C_ID:C_ID + P] = i == j
    own = np.where(j <= i, 0.0, MASKED)
    k[:, C_FULL + P:C_FULL + 2 * P] = own
    k[:, C_BAND:C_BAND + P] = np.where(j > i, 0.0, MASKED)
    k[:, C_BAND + P:C_BAND + 2 * P] = own
    half = ROPE // 2
    inv = (1.0 / (np.float32(10000.0) ** (np.arange(0, ROPE, 2, dtype=np.float32) / np.float32(ROPE)))).astype(np.float32)
    for t in range(TB):
        ang = (np.arange(t * P, (t + 1) * P, dtype=np.float32)[:, None] * inv[None, :]).astype(np.float32)
        k[:, C_COS + t * half:C_COS + (t + 1) * half] = np.cos(ang)
        k[:, C_SIN + t * half:C_SIN + (t + 1) * half] = np.sin(ang)
    k[:, C_IOTA:C_IOTA + NCAND] = np.arange(NCAND)
    k[:, C_ONES:C_ONES + P] = 1.0
    k[:, C_HALF:C_HALF + 2] = -0.5
    return k


_INS = ["x", "c", "w_ada", "b_ada", "w_in", "g_q", "w_uq", "g_kv", "w_ukv", "w_dw", "b_dw", "g_conv", "b_conv",
        "w_pw", "b_pw", "sinks", "w_o", "g_ln1", "b_ln1", "w_pq", "sub_keys", "u_tab", "v_tab", "g_ln2", "b_ln2"]


def kernel(**inputs):
    import numpy as _np
    import concourse.bacc as _bacc
    from concourse import mybir as _mybir
    from concourse.bass_utils import run_bass_kernel_spmd as _run

    nc = _bacc.Bacc("TRN2", target_bir_lowering=False, num_devices=1)
    arrays, args = {}, []
    for name in _INS:
        a = _np.ascontiguousarray(inputs[name])
        arrays[f"in_{name}"] = a
        args.append(nc.dram_tensor(f"in_{name}", a.shape, _mybir.dt.from_np(a.dtype), kind="ExternalInput").ap())
    k = shape_constants(_np)
    arrays["in_consts"] = k
    args.append(nc.dram_tensor("in_consts", k.shape, _mybir.dt.float32, kind="ExternalInput").ap())
    args.append(nc.dram_tensor("out_0", (1, SEQ, D), _mybir.dt.float32, kind="ExternalOutput").ap())
    build(nc, *args)
    r = _run(nc, [arrays], core_ids=[0])
    return r.results[0]["out_0"]
```
